# Optimizing a Trainium2 kernel written in Bass

```python
import functools
import jax, jax.numpy as jnp
from jax import lax
import numpy as np

D_MODEL = 1024
BATCH = 1
SEQ = 1024
DEPTH = 1
DEC_BATCH = 1
DEC_SEQ = 64
PAST_LEN = 256

CHUNK = 64
N_META = 16
EPS = 1e-6
MLA_HEADS = 8
Q_LORA_RANK = 256
KV_LORA_RANK = 128
QK_NOPE_DIM = 64
ROPE_DIM = 32
V_HEAD_DIM = 64
ROPE_THETA = 10000.0
MLA_WIDTH = MLA_HEADS * V_HEAD_DIM
SM_SCALE = (QK_NOPE_DIM + ROPE_DIM) ** -0.5
Q_BLOCK = 128
HG_HEADS = 4
HG_KEY_DIM = 128
HG_VAL_DIM = 128
HG_KEY_WIDTH = HG_HEADS * HG_KEY_DIM
HG_WIDTH = HG_HEADS * HG_VAL_DIM
HG_BLOCK = 16
MIX_WIDTH = MLA_WIDTH + HG_WIDTH
IN_SPLITS = (Q_LORA_RANK, KV_LORA_RANK, ROPE_DIM, HG_KEY_WIDTH, HG_KEY_WIDTH, HG_WIDTH, HG_WIDTH)
IN_WIDTH = sum(IN_SPLITS)
N_GROUPS = 4
EXPERTS_PER_GROUP = 4
N_EXPERTS = N_GROUPS * EXPERTS_PER_GROUP
TOP_K = 2
EXPERT_FF = 256

kernel_name = 'hymba_mla_hgrn2_hmoe_stream'

def _rmsnorm(x, w):
    xf = x.astype(jnp.float32)
    y = xf * lax.rsqrt(jnp.mean(xf * xf, axis=-1, keepdims=True) + EPS)
    return (y * w.astype(jnp.float32)).astype(x.dtype)

def _rope(x, pos):
    half = ROPE_DIM // 2
    inv = ROPE_THETA ** (-jnp.arange(half, dtype=jnp.float32) / half)
    ang = pos.astype(jnp.float32)[:, None] * inv[None, :]
    cos = jnp.cos(ang)[None, :, None, :]
    sin = jnp.sin(ang)[None, :, None, :]
    xf = x.astype(jnp.float32)
    x1, x2 = xf[..., :half], xf[..., half:]
    return jnp.concatenate([x1 * cos - x2 * sin, x2 * cos + x1 * sin], axis=-1).astype(x.dtype)

def _chunk_ids(n):
    i = np.arange(n)
    return np.where(i < N_META, 0, 1 + (i - N_META) // CHUNK)

def _attend_prompt(q_lat, q_rope, ckv, krope):
    n = q_lat.shape[1]
    cid = _chunk_ids(n)
    outs = []
    for start in range(0, n, Q_BLOCK):
        stop = min(start + Q_BLOCK, n)
        kend = min(n, N_META + int(cid[stop - 1]) * CHUNK)
        ck, kr = ckv[:, :kend], krope[:, :kend]
        s = (jnp.einsum('bqhc,bkc->bhqk', q_lat[:, start:stop], ck)
             + jnp.einsum('bqhr,bkr->bhqk', q_rope[:, start:stop], kr)).astype(jnp.float32) * SM_SCALE
        mask = jnp.asarray(cid[start:stop, None] >= cid[None, :kend])
        p = jax.nn.softmax(jnp.where(mask[None, None], s, -jnp.inf), axis=-1).astype(ck.dtype)
        outs.append(jnp.einsum('bhqk,bkc->bqhc', p, ck))
    return jnp.concatenate(outs, axis=1)

def _attend_sample(cache_ckv, cache_krope, q_lat, q_rope, ckv, krope):
    ck = jnp.concatenate([cache_ckv.astype(ckv.dtype), ckv], axis=1)
    kr = jnp.concatenate([cache_krope.astype(krope.dtype), krope], axis=1)
    s = (jnp.einsum('bqhc,bkc->bhqk', q_lat, ck)
         + jnp.einsum('bqhr,bkr->bhqk', q_rope, kr)).astype(jnp.float32) * SM_SCALE
    p = jax.nn.softmax(s, axis=-1).astype(ck.dtype)
    return jnp.einsum('bhqk,bkc->bqhc', p, ck)

def _gated_scan(q, k, v, logf, s0):
    B, T, H, K = q.shape
    L = HG_BLOCK
    Tp = ((T + L - 1) // L) * L
    pad = ((0, 0), (0, Tp - T), (0, 0), (0, 0))
    q, k, v, logf = (jnp.pad(a, pad) for a in (q, k, v, logf))
    n = Tp // L
    blocks = lambda a: a.reshape(B, n, L, H, a.shape[-1]).swapaxes(0, 1)
    causal = jnp.tril(jnp.ones((L, L), dtype=bool))[None, :, :, None, None]

    def step(S, blk):
        qb, kb, vb, gb = blk
        b = jnp.cumsum(gb, axis=1)
        o_inter = jnp.einsum('bthk,bhkv->bthv', qb * jnp.exp(b), S)
        decay = jnp.exp(jnp.where(causal, b[:, :, None] - b[:, None, :], -jnp.inf))
        attn = jnp.einsum('bthk,bshk,btshk->bhts', qb, kb, decay)
        o_intra = jnp.einsum('bhts,bshv->bthv', attn, vb)
        bL = b[:, -1]
        S_new = jnp.exp(bL)[..., None] * S + jnp.einsum('bshk,bshv->bhkv', kb * jnp.exp(bL[:, None] - b), vb)
        return S_new, o_inter + o_intra

    S_fin, o = lax.scan(step, s0, (blocks(q), blocks(k), blocks(v), blocks(logf)))
    o = o.swapaxes(0, 1).reshape(B, Tp, H, v.shape[-1])[:, :T]
    return o, S_fin

def _hgrn2(hq, hf, hi, hg, lb, gnorm, s0):
    B, S, _ = hq.shape
    heads = lambda a: a.reshape(B, S, HG_HEADS, -1)
    q = jax.nn.silu(hq.astype(jnp.float32)) * (HG_KEY_DIM ** -0.5)
    f = lb + (1.0 - lb) * jax.nn.sigmoid(hf.astype(jnp.float32))
    k = 1.0 - f
    o, s_new = _gated_scan(heads(q), heads(k), heads(hi.astype(jnp.float32)), heads(jnp.log(f)),
                           s0.astype(jnp.float32))
    o = o * lax.rsqrt(jnp.mean(o * o, axis=-1, keepdims=True) + EPS) * gnorm.astype(jnp.float32)
    o = o * jax.nn.silu(heads(hg.astype(jnp.float32)))
    return o.reshape(B, S, HG_WIDTH).astype(hq.dtype), s_new.astype(hq.dtype)

def _hier_moe(x, w_rg, b_rg, w_re, b_re, w1, w3, w2):
    B, S, D = x.shape
    t = x.reshape(-1, D)
    p_group = jax.nn.softmax((t @ w_rg).astype(jnp.float32) + b_rg.astype(jnp.float32), axis=-1)
    g_top, g_idx = lax.top_k(p_group, 1)
    e_logits = ((t @ w_re).astype(jnp.float32) + b_re.astype(jnp.float32)).reshape(-1, N_GROUPS, EXPERTS_PER_GROUP)
    e_sel = jnp.take_along_axis(e_logits, g_idx[:, :, None], axis=1)[:, 0]
    e_top, e_idx = lax.top_k(jax.nn.softmax(e_sel, axis=-1), TOP_K)
    e_w = e_top / jnp.sum(e_top, axis=-1, keepdims=True)
    within = jnp.sum(jax.nn.one_hot(e_idx, EXPERTS_PER_GROUP, dtype=jnp.float32) * e_w[..., None], axis=1)
    gates = (jax.nn.one_hot(g_idx[:, 0], N_GROUPS, dtype=jnp.float32)[:, :, None]
             * within[:, None, :] * g_top[:, :, None]).reshape(-1, N_EXPERTS)
    y = jnp.zeros(t.shape, jnp.float32)
    for e in range(N_EXPERTS):
        he = jax.nn.silu(t @ w1[e]) * (t @ w3[e])
        y = y + gates[:, e:e + 1] * (he @ w2[e]).astype(jnp.float32)
    return y.reshape(B, S, D).astype(x.dtype)

def _layer(h, pos, attend, s0, lb, attn_norm, w_in, q_norm, kv_norm, w_uq, w_uk, w_uv, hg_gnorm, w_o,
           ffn_norm, w_rg, b_rg, w_re, b_re, w1, w3, w2):
    B, S, _ = h.shape
    hn = _rmsnorm(h, attn_norm)
    z = hn @ w_in
    cq, ckv_pre, kr_pre, hq, hf, hi, hg = jnp.split(z, np.cumsum(IN_SPLITS)[:-1].tolist(), axis=-1)
    q = jnp.einsum('bsc,chd->bshd', _rmsnorm(cq, q_norm), w_uq)
    q_rope = _rope(q[..., QK_NOPE_DIM:], pos)
    q_lat = jnp.einsum('bshn,chn->bshc', q[..., :QK_NOPE_DIM], w_uk)
    ckv = _rmsnorm(ckv_pre, kv_norm)
    krope = _rope(kr_pre[:, :, None, :], pos)[:, :, 0, :]
    o_lat = attend(q_lat, q_rope, ckv, krope)
    o_mla = jnp.einsum('bshc,chv->bshv', o_lat, w_uv).reshape(B, S, MLA_WIDTH)
    o_hg, s_new = _hgrn2(hq, hf, hi, hg, lb, hg_gnorm, s0)
    h = h + jnp.concatenate([o_mla, o_hg], axis=-1) @ w_o
    h = h + _hier_moe(_rmsnorm(h, ffn_norm), w_rg, b_rg, w_re, b_re, w1, w3, w2)
    return h, ckv, krope, s_new

def setup_inputs(seed: int = 0) -> dict:
    key = jax.random.key(seed)
    ks = jax.random.split(key, 26)
    f32 = jnp.float32
    nrm = lambda k, shape, scale: jax.random.normal(k, shape, f32) * scale
    gain = lambda k, shape: 1.0 + 0.01 * jax.random.normal(k, shape, f32)
    return {
        'x_prompt': nrm(ks[0], (BATCH, SEQ, D_MODEL), 1.0),
        'x_sample': nrm(ks[1], (DEC_BATCH, DEC_SEQ, D_MODEL), 1.0),
        'cache_ckv': nrm(ks[2], (DEPTH, DEC_BATCH, PAST_LEN, KV_LORA_RANK), 1.0),
        'cache_krope': nrm(ks[3], (DEPTH, DEC_BATCH, PAST_LEN, ROPE_DIM), 1.0),
        'state_hgrn': nrm(ks[4], (DEPTH, DEC_BATCH, HG_HEADS, HG_KEY_DIM, HG_VAL_DIM), 0.3),
        'meta_tokens': nrm(ks[5], (N_META, D_MODEL), 1.0),
        'attn_norm': gain(ks[6], (DEPTH, D_MODEL)),
        'w_in': nrm(ks[7], (DEPTH, D_MODEL, IN_WIDTH), D_MODEL ** -0.5),
        'q_norm': gain(ks[8], (DEPTH, Q_LORA_RANK)),
        'kv_norm': gain(ks[9], (DEPTH, KV_LORA_RANK)),
        'w_uq': nrm(ks[10], (DEPTH, Q_LORA_RANK, MLA_HEADS, QK_NOPE_DIM + ROPE_DIM), Q_LORA_RANK ** -0.5),
        'w_uk': nrm(ks[11], (DEPTH, KV_LORA_RANK, MLA_HEADS, QK_NOPE_DIM), KV_LORA_RANK ** -0.5),
        'w_uv': nrm(ks[12], (DEPTH, KV_LORA_RANK, MLA_HEADS, V_HEAD_DIM), KV_LORA_RANK ** -0.5),
        'hg_lb_logits': nrm(ks[13], (DEPTH + 1, HG_KEY_WIDTH), 0.1),
        'hg_gnorm': gain(ks[14], (DEPTH, HG_VAL_DIM)),
        'w_o': nrm(ks[15], (DEPTH, MIX_WIDTH, D_MODEL), MIX_WIDTH ** -0.5),
        'ffn_norm': gain(ks[16], (DEPTH, D_MODEL)),
        'w_router_group': nrm(ks[17], (DEPTH, D_MODEL, N_GROUPS), D_MODEL ** -0.5),
        'b_router_group': nrm(ks[18], (DEPTH, N_GROUPS), 0.01),
        'w_router_expert': nrm(ks[19], (DEPTH, D_MODEL, N_EXPERTS), D_MODEL ** -0.5),
        'b_router_expert': nrm(ks[20], (DEPTH, N_EXPERTS), 0.01),
        'w1': nrm(ks[21], (DEPTH, N_EXPERTS, D_MODEL, EXPERT_FF), D_MODEL ** -0.5),
        'w3': nrm(ks[22], (DEPTH, N_EXPERTS, D_MODEL, EXPERT_FF), D_MODEL ** -0.5),
        'w2': nrm(ks[23], (DEPTH, N_EXPERTS, EXPERT_FF, D_MODEL), EXPERT_FF ** -0.5),
        'final_norm': gain(ks[24], (D_MODEL,)),
    }

def reference(x_prompt, x_sample, cache_ckv, cache_krope, state_hgrn, meta_tokens, attn_norm, w_in, q_norm,
              kv_norm, w_uq, w_uk, w_uv, hg_lb_logits, hg_gnorm, w_o, ffn_norm, w_router_group, b_router_group,
              w_router_expert, b_router_expert, w1, w3, w2, final_norm):
    lb_all = jnp.cumsum(jax.nn.softmax(hg_lb_logits.astype(jnp.float32), axis=0), axis=0)
    b_p = x_prompt.shape[0]
    hp = jnp.concatenate([jnp.broadcast_to(meta_tokens.astype(x_prompt.dtype)[None], (b_p, N_META, D_MODEL)),
                          x_prompt], axis=1)
    hs = x_sample
    pos_p = jnp.arange(hp.shape[1])
    pos_s = PAST_LEN + jnp.arange(hs.shape[1])
    s0_p = jnp.zeros((b_p, HG_HEADS, HG_KEY_DIM, HG_VAL_DIM), jnp.float32)
    ckv_p, kr_p, st_p, ckv_s, kr_s, st_s = [], [], [], [], [], []
    for l in range(DEPTH):
        wts = (lb_all[l], attn_norm[l], w_in[l], q_norm[l], kv_norm[l], w_uq[l], w_uk[l], w_uv[l], hg_gnorm[l],
               w_o[l], ffn_norm[l], w_router_group[l], b_router_group[l], w_router_expert[l],
               b_router_expert[l], w1[l], w3[l], w2[l])
        hp, c1, r1, s1 = _layer(hp, pos_p, _attend_prompt, s0_p, *wts)
        hs, c2, r2, s2 = _layer(hs, pos_s, functools.partial(_attend_sample, cache_ckv[l], cache_krope[l]),
                                state_hgrn[l], *wts)
        ckv_p.append(c1); kr_p.append(r1); st_p.append(s1)
        ckv_s.append(c2); kr_s.append(r2); st_s.append(s2)
    y_prompt = _rmsnorm(hp[:, N_META:], final_norm)
    y_sample = _rmsnorm(hs, final_norm)
    return (y_prompt, y_sample, jnp.stack(ckv_p), jnp.stack(kr_p), jnp.stack(st_p),
            jnp.stack(ckv_s), jnp.stack(kr_s), jnp.stack(st_s))


_drawn_inputs = setup_inputs


def setup_inputs(seed=0):
    import zlib

    import numpy as np

    out = dict(_drawn_inputs(seed))
    spreads = {}
    factors = {'q_norm': 5.819,
     'kv_norm': 5.06,
     'hg_gnorm': 23.184,
     'b_router_group': 21.538,
     'b_router_expert': 29.504,
     'final_norm': 32.319,
     'cache_ckv': 8.0,
     'cache_krope': 8.0,
     'state_hgrn': 3.355,
     'ffn_norm': 8.0}
    for name, (base, spread) in spreads.items():
        noise = np.random.default_rng([zlib.crc32(name.encode()), seed]).standard_normal(out[name].shape)
        drawn = base * np.exp(spread * noise) if base else spread * noise
        out[name] = __import__('jax').numpy.asarray(drawn.astype(out[name].dtype))
    for name, factor in factors.items():
        out[name] = (out[name] * factor).astype(out[name].dtype)
    return out
```

```python
from contextlib import ExitStack

import concourse.bass as bass
from concourse import mybir

F32 = mybir.dt.float32
I32 = mybir.dt.int32
ALU = mybir.AluOpType
ACT = mybir.ActivationFunctionType
AX = mybir.AxisListType

P = 128
D = 1024
KC = D // P
NT = 9
LAST = 8
SAMPLE, META = 64, 16
ROWS = [P] * 8 + [SAMPLE + META]
T = 8 * P + SAMPLE + META
TP = NT * P
ORDER = [LAST] + list(range(8))
EPS = 1e-6
QR, CR, RD = 256, 128, 32
NOPE, VD, MH = 64, 64, 8
QD = NOPE + RD
SCALE = float(QD) ** -0.5
ZA = QR + CR + RD
HH, HK = 4, 128
HW = HH * HK
QSCALE = float(HK) ** -0.5
NG, EG, NE, FF = 4, 4, 16, 256
PAST = 256
KB = NT + PAST // P
SLOT_TILES = (2 * T) // P + NE
SLOTS = SLOT_TILES * P
NEG = -1e30
LEVELS = [1, 2, 4, 8, 16, 32, 64]

C_ID = 0
C_IDQ = C_ID + P
C_BD = C_IDQ + P
C_TRI = C_BD + HW
C_ONE = C_TRI + P
C_COS = C_ONE + P
C_SIN = C_COS + NT * 16
C_W4 = C_SIN + NT * 16
C_THR = C_W4 + 4
C_IOTA = C_THR + 9
C_VALID = C_IOTA + SLOT_TILES
C_TOK = C_VALID + NT
C_HALF = C_TOK + NT
C_END = C_HALF + NT * 4


def constants():
    import numpy as np
    c = np.zeros((P, C_END), np.float32)
    c[:, C_ID:C_ID + P] = np.eye(P)
    c[:, C_IDQ:C_IDQ + P] = np.eye(P) * QSCALE
    c[:, C_BD:C_BD + HW] = (np.arange(P)[:, None] // META == np.arange(HW)[None] // VD)
    c[:, C_TRI:C_TRI + P] = np.triu(np.ones((P, P)), 1)
    c[:, C_ONE:C_ONE + P] = 1.0
    pos = np.zeros((NT, P), np.float32)
    for t in range(8):
        pos[t] = META + t * P + np.arange(P)
    pos[LAST, :SAMPLE] = PAST + np.arange(SAMPLE)
    pos[LAST, SAMPLE:SAMPLE + META] = np.arange(META)
    inv = (np.float32(10000.0) ** (-np.arange(16, dtype=np.float32) / np.float32(16))).astype(np.float32)
    ang = (pos[:, :, None] * inv).astype(np.float32).transpose(1, 0, 2).reshape(P, NT * 16)
    c[:, C_COS:C_COS + NT * 16] = np.cos(ang.astype(np.float64))
    c[:, C_SIN:C_SIN + NT * 16] = np.sin(ang.astype(np.float64))
    c[:, C_W4:C_W4 + 4] = [4, 3, 2, 1]
    c[:, C_THR:C_THR + 9] = np.arange(9) * P
    c[:, C_IOTA:C_IOTA + SLOT_TILES] = np.arange(SLOT_TILES)
    for t in range(NT):
        c[:ROWS[t], C_VALID + t] = 1.0
        c[:, C_TOK + t] = t * P + np.arange(P)
    c[:, C_HALF:C_END] = -0.5
    m = np.zeros((P, len(LEVELS), 64), np.int32)
    s = np.arange(P)[:, None]
    for n, h in enumerate(LEVELS):
        k = np.arange(64)[None]
        t = (k // h) * 2 * h + h + k % h
        m[:, n] = (s // (2 * h) == t // (2 * h)) & (s % (2 * h) < h)
    return c, m.reshape(P, -1)


def hybrid_layer(nc, x_prompt, x_sample, cache_ckv, cache_krope, state_hgrn, meta_tokens, attn_norm, w_in, q_norm,
                 kv_norm, w_uq, w_uk, w_uv, hg_lb_logits, hg_gnorm, w_o, ffn_norm, w_router_group, b_router_group,
                 w_router_expert, b_router_expert, w1, w3, w2, final_norm, table, level_masks,
                 y_prompt, y_sample, ckv_prompt, krope_prompt, hgrn_prompt, ckv_sample, krope_sample, hgrn_sample):
    ctx = ExitStack()
    arena_floats = 53000
    arena = ctx.enter_context(nc.sbuf_tensor("arena", [P, arena_floats], F32))
    ps = ctx.enter_context(nc.psum_tensor("ps", [P, 8, 512], F32))

    class Region:
        def __init__(self, base):
            self.at = base

        def take(self, *dims):
            n = 1
            for d in dims:
                n *= d
            a = arena[:, self.at:self.at + n]
            self.at += n
            assert self.at <= arena_floats, self.at
            if len(dims) == 2:
                a = a.rearrange("p (a b) -> p a b", a=dims[0])
            if len(dims) == 3:
                a = a.rearrange("p (a b c) -> p a b c", a=dims[0], b=dims[1])
            return a

    def sem(name):
        return ctx.enter_context(nc.semaphore(name))

    keep = Region(0)
    tab = keep.take(C_END)
    masks = keep.take(len(LEVELS) * 64).bitcast(I32)
    logits = keep.take(NT, NG + NE)
    stat = keep.take(64)
    hg_out = keep.take(NT, HW)
    z_mla = keep.take(NT, ZA)
    ident = tab[:, C_ID:C_ID + P]
    ident_q = tab[:, C_IDQ:C_IDQ + P]
    ones = tab[:, C_ONE:C_ONE + P]
    neg_half = tab[:, C_HALF:C_HALF + NT * 4]

    r = Region(keep.at)
    v_hg = r.take(NT, HW)
    q_hg = r.take(HH, TP)
    f_hg = r.take(HH, TP)
    norm_base = r.at
    k_hg = r.take(HH, TP)
    gn_b = r.take(HK)
    lbl = r.take(2, HH)
    lb = r.take(4, HH)
    work_base = r.at
    x_t = r.take(KC, T)
    w_grp = r.take(2, KC, 512)
    r = Region(norm_base)
    x_row = r.take(2, D)
    xs = r.take(1, D)
    an_b = r.take(D)
    r = Region(work_base)
    q_lv = r.take(3, HH, P)
    k_lv = r.take(3, HH, P)
    tot = r.take(8, HH, 64)
    attn_t = r.take(2, HH, P)
    state = r.take(HH, HK)
    state_s = r.take(HH, HK)
    k_rows = r.take(HH, P)
    o_stat = r.take(2, HH)
    o_rstd = r.take(2, HH)

    r = Region(keep.at)
    k_t = r.take(MH, T + PAST)
    v_rows = r.take(KB, MH * VD)
    v_meta = r.take(MH * VD)
    ckv_t = r.take(T + PAST)
    cq_t = r.take(2, TP)
    wuq = r.take(2, MH * QD)
    wuk = r.take(MH * NOPE)
    wuv = r.take(MH * VD)
    wo = r.take(KC, D)
    wr = r.take(KC, NG + NE)
    br_b = r.take(NG + NE)
    fn_b = r.take(D)
    q_t = r.take(MH, P)
    q_row = r.take(MH, QD)
    rope_tmp = r.take(4, NT * 16)
    p_base = r.at
    p_rows = r.take(3, D)
    p_t = r.take(2, 4, P)
    pm_row = r.take(MH, META)
    nbias = r.take(2, MH)
    sm_stat = r.take(6, MH)
    h_base = r.at
    h_row = r.take(2, D)
    h_stat = r.take(2, 2)
    hn_row = r.take(D)
    r = Region(keep.at - NT * ZA)
    hn_t = r.take(KC, P)
    mix_t = r.take(KC, P)
    mix_row = r.take(HW)
    r = Region(p_base)
    kr96 = r.take(KB, 96)
    cache_c = r.take(2, CR)
    m8 = r.take(P)
    z_sq = r.take(NT, 2)
    r = Region(h_base)
    qn_b = r.take(QR)
    kvn_b = r.take(CR)
    z_junk = r.take(QR)

    r = Region(keep.at - NT * ZA)
    rt = r.take(24, NT * NE)
    expert_of = r.take(SLOT_TILES).bitcast(I32)
    gates = r.take(2, NT)
    slot_i = r.take(2, NT).bitcast(I32)
    tok_rows = r.take(P)
    tok_i = r.take(SLOT_TILES).bitcast(I32)
    w13_e = r.take(3, KC, 2 * FF)
    w2_e = r.take(3, 2, D)
    xg = r.take(3, D)
    xg_t = r.take(KC, P)
    act_h = r.take(FF)
    g_row = r.take(FF)
    g_t = r.take(2, P)
    y_row = r.take(3, D)
    r = Region(keep.at + 8000)
    res = r.take(2, D)
    ya = r.take(2, D)
    yb = r.take(2, D)
    y_out = r.take(2, D)
    fin_b = r.take(D)
    y_sq = r.take(D)
    y_stat = r.take(2, NT)

    h1_dram = nc.dram_tensor("h1_dram", [T, D], F32).ap()
    hn_dram = nc.dram_tensor("hn_dram", [T, D], F32).ap()
    tok_dram = nc.dram_tensor("tok_dram", [SLOTS, 1], F32).ap()
    y_dram = nc.dram_tensor("y_dram", [SLOTS, D], F32).ap()

    phase_end = sem("phase_end")
    phases = {"n": 0}

    def end_phase(eng, n):
        eng.drain().then_inc(phase_end, 1)
        eng.wait_ge(phase_end, 4 * (n + 1))

    s_tab = sem("s_tab")
    s_xrow = [sem(f"s_xrow{i}") for i in range(2)]
    s_norm_w = sem("s_norm_w")
    s_ssq = sem("s_ssq")
    s_rstd = sem("s_rstd")
    s_xs = sem("s_xs")
    s_xps = sem("s_xps")
    s_xta = sem("s_xta")
    s_xtv = sem("s_xtv")
    s_wg = [sem(f"s_wg{i}") for i in range(2)]
    s_zps = sem("s_zps")
    s_zev = sem("s_zev")
    s_zero = sem("s_zero")
    s_lb = sem("s_lb")
    s_lbe = sem("s_lbe")
    s_fk = sem("s_fk")
    s_gs = sem("s_gs")

    c0 = ZA
    GROUPS = [("mla", 0, ZA), ("v", c0 + 2 * HW, HW), ("gate", c0 + 3 * HW, HW), ("f", c0 + HW, HW), ("q", c0, HW)]
    Z_OUT = []
    for g, (kind, _, _) in enumerate(GROUPS):
        if kind in ("f", "q"):
            Z_OUT += [(kind, g, m, n) for m in range(HH) for n in range(3)]
        else:
            Z_OUT += [(kind, g, t, 0) for t in range(NT)]
    ZN = T // 3
    Z_RING = 6

    s_hin = sem("s_hin")
    s_init = sem("s_init")
    s_lvl = sem("s_lvl")
    s_cpy = sem("s_cpy")
    s_prod = sem("s_prod")
    s_mask = sem("s_mask")
    s_ops = sem("s_ops")
    s_osq = sem("s_osq")
    s_ors = sem("s_ors")
    s_oev = sem("s_oev")
    s_ktp = sem("s_ktp")
    s_kte = sem("s_kte")
    s_sps = sem("s_sps")
    s_sev = sem("s_sev")
    s_st0 = sem("s_st0")

    s_out = sem("s_out")
    outs = {"n": 0}


    def col0(t):
        return t * P

    def levels(c):
        return LEVELS[:6] if c == LAST else LEVELS

    LV0 = [sum(len(levels(c)) for c in ORDER[:i]) for i in range(NT + 1)]
    PR0 = [sum(len(levels(c)) + 1 for c in ORDER[:i]) for i in range(NT + 1)]

    def x_half(act, t):
        act.wait_ge(s_xps, 2 * t + 1)
        act.activation(x_t[:, 0:4, col0(t):col0(t) + ROWS[t]],
                       ps[:, 6, :].rearrange("p (a b) -> p a b", a=4)[:, :, 0:ROWS[t]], ACT.Copy).then_inc(s_xta, 1)

    s_pool = sem("s_pool")
    pool_chain = [0]
    s_dve = sem("s_dve")
    dve_chain = [0]

    def key_col(kb):
        return kb * P if kb < NT else T + (kb - NT) * P

    def key_rows(kb):
        return ROWS[kb] if kb < NT else P

    MCOL = LAST * P + SAMPLE

    def main_blocks(t):
        return [(NT, P), (NT + 1, P), (LAST, SAMPLE)] if t == LAST else [(kb, P) for kb in range(t + 1)]

    def main_width(t):
        return sum(w for _, w in main_blocks(t))

    STEPS = [("kb", kb, 0) for kb in range(KB)]
    KN = [(0, 512), (512, 512), (1024, T + PAST - 1024)]
    STEPS += [("kn", hd, n) for hd in range(MH) for n in range(3)]
    STEPS += [("v", kb, 0) for kb in range(KB)] + [("vm", 0, 0), ("q", 0, 0), ("qt", 0, 0)]
    for i in range(NT):
        STEPS.append(("meta", i, 0))
        for hd in range(MH):
            STEPS.append(("score", i, hd))
            side = {1: "wot", 2: "wo", 3: "sq", 4: "hn", 5: "hnt", 6: "rt"}.get(hd)
            if i and side:
                STEPS.append((side, i - 1, 0))
            if hd == 3 and i + 1 < NT:
                STEPS.append(("q", i + 1, 0))
            if hd >= 2:
                STEPS.append(("attn", i, hd - 2))
        STEPS += [("attn", i, 6), ("attn", i, 7), ("mpv", i, 0)]
        if i + 1 < NT:
            STEPS.append(("qt", i + 1, 0))
    STEPS += [(s, NT - 1, 0) for s in ("wot", "wo", "sq", "hn", "hnt", "rt")]

    STEPS_ACT = []
    held = None
    for st in STEPS:
        if st[0] == "score" and st[2] >= 2:
            held = st
            continue
        STEPS_ACT.append(st)
        if st[0] == "attn" and held:
            STEPS_ACT.append(held)
            held = None

    S_JOB = {}
    PT_GROUP = {}
    P_INDEX = {}
    for st in STEPS:
        kind, i, hd = st
        if kind in ("kn", "v", "vm", "q", "score", "wo", "rt"):
            S_JOB[st] = len(S_JOB)
        if kind == "kb":
            PT_GROUP[st + (0,)] = len(PT_GROUP)
        if kind in ("qt", "wot", "hnt"):
            for half in range(2):
                PT_GROUP[st + (half,)] = len(PT_GROUP)
        if kind == "attn":
            for g in range((len(main_blocks(ORDER[i])) + 3) // 4):
                PT_GROUP[st + (g,)] = len(PT_GROUP)
                P_INDEX[st + (g,)] = len(P_INDEX)
        if kind == "mpv":
            PT_GROUP[st + (0,)] = len(PT_GROUP)
            P_INDEX[st + (0,)] = len(P_INDEX)

    def last_group(a):
        i, hd = divmod(a, MH)
        return PT_GROUP[("attn", i, hd, (len(main_blocks(ORDER[i])) + 3) // 4 - 1)]

    s_wat = sem("s_wat")
    s_nw = sem("s_nw")
    s_cch = sem("s_cch")
    s_zsq = sem("s_zsq")
    s_zrs = sem("s_zrs")
    s_kr0 = sem("s_kr0")
    s_zn = sem("s_zn")
    s_sps2 = sem("s_sjob")
    s_srel = [sem(f"s_srel{i}") for i in range(2)]
    s_pt = sem("s_pt")
    s_ptrel = [sem(f"s_ptrel{i}") for i in range(2)]
    s_m8 = sem("s_m8")
    s_kv_out = sem("s_kv_out")
    s_qrope = sem("s_qrope")
    s_meta = sem("s_meta")
    s_nb = sem("s_nb")
    s_pused = sem("s_pused")
    s_dm = sem("s_dm")
    s_pm = sem("s_pm")
    s_o = sem("s_o")
    s_mix = sem("s_mix")
    s_xres = [sem(f"s_xres{i}") for i in range(2)]
    s_h1st = sem("s_h1st")
    s_hsq = sem("s_hsq")
    s_hrs = sem("s_hrs")
    s_hn = sem("s_hn")
    s_hnst = sem("s_hnst")

    def s_banks(st):
        return 2 * (S_JOB[st] % 2)

    def s_wait_free(pe, st):
        k = S_JOB[st]
        if k >= 2:
            pe.wait_ge(s_srel[k % 2], k // 2)

    def s_wait_read(eng, st):
        k = S_JOB[st]
        eng.wait_ge(s_srel[k % 2], k // 2 + 1)

    def pt_wait_free(pe, key):
        k = PT_GROUP[key]
        if k >= 2:
            pe.wait_ge(s_ptrel[k % 2], k // 2)

    def pt_wait_done(eng, key):
        k = PT_GROUP[key]
        eng.wait_ge(s_ptrel[k % 2], k // 2 + 1)

    def copies_it(key, who):
        return (PT_GROUP[key] % 2 == 0) == (who == "act")

    def evacuate(eng, who, st):
        kind, i, hd = st
        t = ORDER[i] if i < NT else 0
        R = ROWS[t]
        cp = (lambda o, a: eng.activation(o, a, ACT.Copy)) if who == "act" else eng.tensor_copy
        keys = [k for k in (st + (g,) for g in range(2)) if k in PT_GROUP]
        for key in keys:
            if not copies_it(key, who):
                continue
            g = PT_GROUP[key]
            eng.wait_ge(s_pt, g + 1)
            src = ps[:, 4 + g % 2, :].rearrange("p (a b) -> p a b", a=4)
            rel = s_ptrel[g % 2]
            half = key[3]
            if kind == "kb":
                n, c = key_rows(i), key_col(i)
                if i < NT:
                    cp(cq_t[:, :, c:c + n], src[:, 0:2, 0:n])
                cp(ckv_t[:, c:c + n], src[:, 2, 0:n])
                cp(k_t[64:96, :, c:c + n], src[64:96, 3, 0:n].unsqueeze(1).to_broadcast([32, MH, n])).then_inc(rel, 1)
            elif kind == "qt":
                cp(q_t[0:QD, 4 * half:4 * half + 4, 0:R], src[0:QD, :, 0:R]).then_inc(rel, 1)
            elif kind in ("wot", "hnt"):
                if kind == "wot":
                    eng.wait_ge(s_kv_out, 16 * 6)
                dst = mix_t if kind == "wot" else hn_t
                cp(dst[:, 4 * half:4 * half + 4, 0:R], src[:, :, 0:R]).then_inc(rel, 1)
            else:
                ip = P_INDEX[key]
                if ip >= 2:
                    eng.wait_ge(s_pused, ip - 1)
                if kind == "mpv":
                    cp(p_t[:, ip % 2, 0, 0:R], src[:, 0, 0:R]).then_inc(rel, 1)
                else:
                    bl = main_blocks(t)[4 * half:4 * half + 4]
                    full = [b for b in bl if b[1] == P]
                    ins = cp(p_t[:, ip % 2, 0:len(full), 0:R], src[:, 0:len(full), 0:R])
                    if len(full) < len(bl):
                        ins = cp(p_t[0:SAMPLE, ip % 2, len(full), 0:R], src[0:SAMPLE, len(full), 0:R])
                    ins.then_inc(rel, 1)

    def attention_loads(sp):
        sp.wait_ge(phase_end, 8)
        sp.dma_start(cache_c, cache_ckv[0, 0].rearrange("(b p) c -> p b c", p=P)).then_inc(s_cch, 16)
        sp.dma_start(kr96[:, NT:KB, 64:96], cache_krope[0, 0].rearrange("(b p) c -> p b c", p=P)).then_inc(s_cch, 16)
        sp.dma_start(qn_b, q_norm[0:1, :].to_broadcast([P, QR])).then_inc(s_nw, 16)
        sp.dma_start(kvn_b, kv_norm[0:1, :].to_broadcast([P, CR])).then_inc(s_nw, 16)
        sp.dma_start(wuk, w_uk[0].rearrange("c h n -> c (h n)")).then_inc(s_wat, 16)
        sp.dma_start(wuv, w_uv[0].rearrange("c h n -> c (h n)")).then_inc(s_wat, 16)
        sp.dma_start(wuq, w_uq[0].rearrange("(c p) h n -> p c (h n)", p=P)).then_inc(s_wat, 16)
        sp.dma_start(wo, w_o[0].rearrange("(c p) n -> p c n", p=P)).then_inc(s_wat, 16)
        sp.dma_start(wr[:, :, 0:NG], w_router_group[0].rearrange("(c p) n -> p c n", p=P),
                     allow_slow_non_contiguous=True).then_inc(s_wat, 16)
        sp.dma_start(wr[:, :, NG:], w_router_expert[0].rearrange("(c p) n -> p c n", p=P),
                     allow_slow_non_contiguous=True).then_inc(s_wat, 16)
        sp.dma_start(br_b[:, 0:NG], b_router_group[0:1, :].to_broadcast([P, NG])).then_inc(s_wat, 16)
        sp.dma_start(br_b[:, NG:], b_router_expert[0:1, :].to_broadcast([P, NE])).then_inc(s_wat, 16)
        sp.dma_start(fn_b, ffn_norm[0:1, :].to_broadcast([P, D])).then_inc(s_wat, 16)
        sp.wait_ge(s_zn, 3)
        lat = z_mla[:, :, QR:QR + CR]
        rop = kr96[:, :, 64:96]
        for dst_p, dst_s, src in ((ckv_prompt, ckv_sample, lat), (krope_prompt, krope_sample, rop)):
            sp.dma_start(dst_p[0, 0, META:, :].rearrange("(t p) c -> p t c", p=P), src[:, 0:8, :]).then_inc(s_kv_out, 16)
            sp.dma_start(dst_p[0, 0, 0:META, :], src[SAMPLE:SAMPLE + META, LAST, :]).then_inc(s_kv_out, 16)
            sp.dma_start(dst_s[0, 0], src[0:SAMPLE, LAST, :]).then_inc(s_kv_out, 16)
        sp.wait_ge(s_kv_out, 16 * 6)

        def load_residual(i):
            t = ORDER[i]
            if t < 8:
                sp.dma_start(h_row[:, i % 2, :], x_prompt[0, t * P:(t + 1) * P, :]).then_inc(s_xres[i % 2], 32)
            else:
                sp.dma_start(h_row[0:SAMPLE, i % 2, :], x_sample[0]).then_inc(s_xres[i % 2], 16)
                sp.dma_start(h_row[SAMPLE:SAMPLE + META, i % 2, :], meta_tokens).then_inc(s_xres[i % 2], 16)

        load_residual(0)
        load_residual(1)
        for i in range(NT):
            t, R = ORDER[i], ROWS[ORDER[i]]
            s_wait_read(sp, ("wo", i, 0))
            sp.dma_start(h1_dram[t * P:t * P + R, :], h_row[0:R, i % 2, :]).then_inc(s_h1st, 16)
            sp.wait_ge(s_hn, i + 1)
            sp.dma_start(hn_dram[t * P:t * P + R, :], hn_row[0:R, :]).then_inc(s_hnst, 16)
            if i + 2 < NT:
                sp.wait_ge(s_h1st, 16 * (i + 1))
                load_residual(i + 2)

    def attention_pool(pool, rsqrt_mean):
        pool.memset(kr96[:, :, 0:64], 0.0).then_inc(s_kr0, 1)
        rsqrt_mean(z_sq.rearrange("p a b -> p (a b)")[:, 0:NT], z_sq.rearrange("p a b -> p (a b)")[:, 0:NT], QR, s_zsq,
                   s_zrs, 2 * NT)
        rsqrt_mean(z_sq.rearrange("p a b -> p (a b)")[:, NT:2 * NT], z_sq.rearrange("p a b -> p (a b)")[:, NT:2 * NT],
                   CR, s_zsq, s_zrs, 2 * NT)
        for i in range(NT):
            R = ROWS[ORDER[i]]
            rsqrt_mean(h_stat[0:R, i % 2, 1:2], h_stat[0:R, i % 2, 0:1], D, s_hsq, s_hrs, i + 1)

    def attention_act(act):
        for t in range(NT):
            if t:
                act.wait_ge(s_zsq, 2 * t)
            act.activation(z_junk[:, 0:QR], z_mla[:, t, 0:QR], ACT.Square,
                           accum_out=z_sq.rearrange("p a b -> p (a b)")[:, t:t + 1]).then_inc(s_zsq, 1)
            act.wait_ge(s_zsq, 2 * t + 1)
            act.activation(z_junk[:, 0:CR], z_mla[:, t, QR:QR + CR], ACT.Square,
                           accum_out=z_sq.rearrange("p a b -> p (a b)")[:, NT + t:NT + t + 1]).then_inc(s_zsq, 1)
        for st in STEPS_ACT:
            kind, i, hd = st
            t = ORDER[i] if i < NT else 0
            R = ROWS[t]
            if kind != "mpv":
                evacuate(act, "act", st)
            if st in S_JOB:
                k = S_JOB[st]
                bank = s_banks(st)
                if kind in ("kn", "v") and k % 2 == 0:
                    act.wait_ge(s_sps2, k + 1)
                    if kind == "kn":
                        c, n = KN[hd]
                        act.activation(k_t[0:64, i, c:c + n], ps[0:64, bank, 0:n], ACT.Copy).then_inc(s_srel[0], 1)
                    else:
                        n = key_rows(i)
                        act.activation(v_rows[0:n, i, :], ps[0:n, bank, :], ACT.Copy).then_inc(s_srel[0], 1)
                if kind == "q":
                    act.wait_ge(s_sps2, k + 1)
                    act.activation(q_row[0:R].rearrange("p (c h) d -> p c (h d)", c=2), ps[0:R, bank:bank + 2, 0:4 * QD],
                                   ACT.Copy).then_inc(s_srel[k % 2], 1)
                if kind == "score":
                    a = i * MH + hd
                    w = main_width(t)
                    act.wait_ge(s_nb, a + 1)
                    if a == 0:
                        act.wait_ge(s_kv_out, 16 * 6)
                    if a >= 3:
                        act.wait_ge(s_pt, last_group(a - 3) + 1)
                    act.activation(p_rows[0:R, a % 3, 0:w],
                                   ps[0:R, bank:bank + 2, :].rearrange("p a b -> p (a b)")[:, 0:w], ACT.Exp,
                                   bias=nbias[0:R, i % 2, hd:hd + 1], scale=SCALE,
                                   accum_out=sm_stat[0:R, 2, hd:hd + 1]).then_inc(s_srel[k % 2], 1)
            if kind == "mpv":
                act.wait_ge(s_dm, i + 1)
                act.activation(pm_row[0:R], pm_row[0:R], ACT.Exp).then_inc(s_pm, 1)
                evacuate(act, "act", st)
            if kind == "sq":
                s_wait_read(act, ("wo", i, 0))
                if i:
                    act.wait_ge(s_hnst, 16 * i)
                    act.wait_ge(s_pt, PT_GROUP[("hnt", i - 1, 0, 1)] + 1)
                act.activation(hn_row[0:R], h_row[0:R, i % 2, :], ACT.Square,
                               accum_out=h_stat[0:R, i % 2, 0:1]).then_inc(s_hsq, 1)

    def attention_pe(pe):
        pending = []

        def turn(key, blocks, waits=()):
            pt_wait_free(pe, key)
            g = PT_GROUP[key]
            for n, (src, rows, width) in enumerate(blocks):
                if src is not None:
                    ins = pe.transpose(ps[0:width, 4 + g % 2, n * P:n * P + rows], src, ident[0:rows, 0:rows])
            return ins.then_inc(s_pt, 1)

        def weigh():
            key = pending.pop(0)
            kind, i, hd, g = key
            t = ORDER[i]
            R = ROWS[t]
            pt_wait_done(pe, key)
            ip = P_INDEX[key]
            if kind == "mpv":
                pe.matmul(ps[0:R, 6, :], p_t[:, ip % 2, 0, 0:R], v_meta, start=False, stop=True,
                          skip_group_check=True).then_inc(s_pused, 1)
                return
            if i and hd == 0 and g == 0:
                pe.wait_ge(s_mix, i)
            for n, (kb, w) in enumerate(main_blocks(t)[4 * g:4 * g + 4]):
                ins = pe.matmul(ps[0:R, 6, hd * VD:(hd + 1) * VD], p_t[0:w, ip % 2, n, 0:R],
                                v_rows[0:w, kb, hd * VD:(hd + 1) * VD],
                                start=hd == 0 and g == 0 and n == 0, stop=False, skip_group_check=True)
            ins.then_inc(s_pused, 1)

        pe.wait_ge(s_zn, 3)
        pe.wait_ge(s_cch, 32)
        for st in STEPS:
            kind, i, hd = st
            t = ORDER[i] if i < NT else 0
            R = ROWS[t]
            if st in S_JOB:
                s_wait_free(pe, st)
                bank = s_banks(st)
            if kind == "kb":
                n = key_rows(i)
                rows = slice(0, n)
                if i < NT:
                    bl = [(z_mla[rows, i, 0:P], n, P), (z_mla[rows, i, P:2 * P], n, P),
                          (z_mla[rows, i, QR:QR + CR], n, P)]
                else:
                    bl = [(None, 0, 0), (None, 0, 0), (cache_c[:, i - NT, :], n, P)]
                turn(st + (0,), bl + [(kr96[rows, i, :], n, 96)])
            if kind == "kn":
                if i == 0 and hd == 0:
                    pe.wait_ge(s_wat, 16 * 9)
                    for kb in range(KB):
                        pt_wait_done(pe, ("kb", kb, 0, 0))
                c, n = KN[hd]
                pe.matmul(ps[0:NOPE, bank, 0:n], wuk[:, i * NOPE:(i + 1) * NOPE], ckv_t[:, c:c + n],
                          start=True, stop=True).then_inc(s_sps2, 1)
            if kind == "v":
                c, n = key_col(i), key_rows(i)
                pe.matmul(ps[0:n, bank, :], ckv_t[:, c:c + n], wuv, start=True, stop=True).then_inc(s_sps2, 1)
            if kind == "vm":
                pe.wait_ge(s_m8, 1)
                pe.matmul(ps[:, bank, :], m8, wuv, start=True, stop=True).then_inc(s_sps2, 1)
            if kind == "q":
                for n in range(2):
                    for kk in range(2):
                        ins = pe.matmul(ps[0:R, bank + n, 0:4 * QD], cq_t[:, kk, col0(t):col0(t) + R],
                                        wuq[:, kk, n * 4 * QD:(n + 1) * 4 * QD], start=kk == 0, stop=kk == 1)
                ins.then_inc(s_sps2, 1)
            if kind == "qt":
                pe.wait_ge(s_qrope, i + 1)
                for half in range(2):
                    turn(st + (half,), [(q_row[0:R, 4 * half + n, :], R, QD) for n in range(4)])
            if kind == "meta":
                pt_wait_done(pe, ("qt", i, 0, 0))
                pt_wait_done(pe, ("qt", i, 0, 1))
                if i:
                    pe.wait_ge(s_dm, i)
                else:
                    for k in range(2):
                        last = max(v for s_, v in S_JOB.items() if s_[0] in ("kn", "v", "vm") and v % 2 == k)
                        pe.wait_ge(s_srel[k], last // 2 + 1)
                for h_ in range(MH):
                    ins = pe.matmul(ps[0:R, 7, h_ * META:(h_ + 1) * META], q_t[0:QD, h_, 0:R],
                                    k_t[0:QD, h_, MCOL:MCOL + META], start=True, stop=True)
                ins.then_inc(s_meta, 1)
            if kind == "score":
                if t == LAST:
                    pe.matmul(ps[0:R, bank, 0:PAST], q_t[0:QD, hd, 0:R], k_t[0:QD, hd, T:T + PAST],
                              start=True, stop=True)
                    ins = pe.matmul(ps[0:R, bank, PAST:PAST + SAMPLE], q_t[0:QD, hd, 0:R],
                                    k_t[0:QD, hd, LAST * P:LAST * P + SAMPLE], start=True, stop=True)
                else:
                    w = main_width(t)
                    for n in range(0, w, 512):
                        m = min(512, w - n)
                        ins = pe.matmul(ps[0:R, bank + n // 512, 0:m], q_t[0:QD, hd, 0:R],
                                        k_t[0:QD, hd, n:n + m], start=True, stop=True)
                ins.then_inc(s_sps2, 1)
            if kind == "attn":
                a = i * MH + hd
                bl = main_blocks(t)
                s_wait_read(pe, ("score", i, hd))
                for g in range((len(bl) + 3) // 4):
                    key = st + (g,)
                    ins = turn(key, [(p_rows[0:R, a % 3, (4 * g + n) * P:(4 * g + n) * P + w], R, w)
                                     for n, (_, w) in enumerate(bl[4 * g:4 * g + 4])])
                    if pending:
                        weigh()
                    pending.append(key)
            if kind == "mpv":
                while pending:
                    weigh()
                pe.wait_ge(s_pm, i + 1)
                turn(st + (0,), [(pm_row[0:R].rearrange("p h m -> p (h m)"), R, P)])
                pending.append(st + (0,))
                weigh()
            if kind == "wot":
                pe.wait_ge(s_mix, i + 1)
                for half in range(2):
                    src = mix_row if half == 0 else hg_out[:, t, :]
                    turn(st + (half,), [(src[0:R, n * P:(n + 1) * P], R, P) for n in range(4)])
            if kind == "wo":
                pt_wait_done(pe, ("wot", i, 0, 0))
                pt_wait_done(pe, ("wot", i, 0, 1))
                for n in range(2):
                    for kc in range(KC):
                        ins = pe.matmul(ps[0:R, bank + n, :], mix_t[:, kc, 0:R], wo[:, kc, n * 512:(n + 1) * 512],
                                        start=kc == 0, stop=kc == KC - 1)
                ins.then_inc(s_sps2, 1)
            if kind == "hnt":
                pe.wait_ge(s_hn, i + 1)
                for half in range(2):
                    turn(st + (half,), [(hn_row[0:R, (4 * half + n) * P:(4 * half + n + 1) * P], R, P)
                                        for n in range(4)])
            if kind == "rt":
                pt_wait_done(pe, ("hnt", i, 0, 0))
                pt_wait_done(pe, ("hnt", i, 0, 1))
                for kc in range(KC):
                    ins = pe.matmul(ps[0:R, bank, 0:NG + NE], hn_t[:, kc, 0:R], wr[:, kc, :],
                                    start=kc == 0, stop=kc == KC - 1)
                ins.then_inc(s_sps2, 1)

    def attention_dve(dve, link):
        dve.wait_ge(s_nw, 32)
        dve.wait_ge(s_zrs, 2)
        dve.wait_ge(s_kr0, 1)
        zq = z_sq.rearrange("p a b -> p (a b)")
        cq, ck = z_mla[:, :, 0:QR], z_mla[:, :, QR:QR + CR]
        link(dve.tensor_tensor(cq, cq, zq[:, 0:NT].unsqueeze(2).to_broadcast([P, NT, QR]), ALU.mult))
        dve.tensor_tensor(cq, cq, qn_b.unsqueeze(1).to_broadcast([P, NT, QR]), ALU.mult).then_inc(s_zn, 1)
        link(dve.tensor_tensor(ck, ck, zq[:, NT:2 * NT].unsqueeze(2).to_broadcast([P, NT, CR]), ALU.mult))
        dve.tensor_tensor(ck, ck, kvn_b.unsqueeze(1).to_broadcast([P, NT, CR]), ALU.mult).then_inc(s_zn, 1)
        c3 = tab[:, C_COS:C_COS + NT * 16].rearrange("p (t r) -> p t r", t=NT)
        s3 = tab[:, C_SIN:C_SIN + NT * 16].rearrange("p (t r) -> p t r", t=NT)

        def rope(x1, x2, cos, sin, o1, o2, n, R, done):
            tm = [rope_tmp[0:R, k, 0:n * 16].rearrange("p (a b) -> p a b", a=n) for k in range(4)]
            dve.tensor_tensor(tm[0], x1, cos, ALU.mult)
            dve.tensor_tensor(tm[1], x2, sin, ALU.mult)
            dve.tensor_tensor(tm[2], x2, cos, ALU.mult)
            link(dve.tensor_tensor(tm[3], x1, sin, ALU.mult))
            dve.tensor_tensor(o1, tm[0], tm[1], ALU.subtract)
            dve.tensor_tensor(o2, tm[2], tm[3], ALU.add).then_inc(done, 1)

        rope(z_mla[:, :, QR + CR:QR + CR + 16], z_mla[:, :, QR + CR + 16:ZA], c3, s3, kr96[:, 0:NT, 64:80],
             kr96[:, 0:NT, 80:96], NT, P, s_zn)
        for st in STEPS:
            kind, i, hd = st
            t = ORDER[i] if i < NT else 0
            R = ROWS[t]
            if kind != "mpv":
                evacuate(dve, "dve", st)
            if st in S_JOB:
                k = S_JOB[st]
                bank = s_banks(st)
                rel = s_srel[k % 2]
                if kind in ("kn", "v") and k % 2 == 1:
                    dve.wait_ge(s_sps2, k + 1)
                    if kind == "kn":
                        c, n = KN[hd]
                        dve.tensor_copy(k_t[0:64, i, c:c + n], ps[0:64, bank, 0:n]).then_inc(rel, 1)
                    else:
                        n = key_rows(i)
                        dve.tensor_copy(v_rows[0:n, i, :], ps[0:n, bank, :]).then_inc(rel, 1)
                if kind == "vm":
                    dve.wait_ge(s_sps2, k + 1)
                    dve.tensor_tensor(v_meta, ps[:, bank, :], tab[:, C_BD:C_BD + HW], ALU.mult).then_inc(rel, 1)
                if kind == "kn" and i == 0 and hd == 0:
                    pt_wait_done(dve, ("kb", LAST, 0, 0))
                    dve.tensor_copy(m8.rearrange("p (h m) -> p h m", h=MH),
                                    ckv_t[:, MCOL:MCOL + META].unsqueeze(1).to_broadcast([P, MH, META])
                                    ).then_inc(s_m8, 1)
                if kind == "q":
                    s_wait_read(dve, st)
                    sm3 = [a[0:R, t, :].unsqueeze(1).to_broadcast([R, MH, 16]) for a in (c3, s3)]
                    q1, q2 = q_row[0:R, :, NOPE:NOPE + 16], q_row[0:R, :, NOPE + 16:QD]
                    rope(q1, q2, sm3[0], sm3[1], q1, q2, MH, R, s_qrope)
                if kind == "score":
                    a = i * MH + hd
                    w = main_width(t)
                    dve.wait_ge(s_sps2, k + 1)
                    if hd == 0:
                        dve.wait_ge(s_meta, i + 1)
                        if t == LAST:
                            link(dve.memset(ps[0:SAMPLE, 7, 0:MH * META], NEG))
                        dve.tensor_reduce(sm_stat[0:R, 1, :],
                                          ps[0:R, 7, 0:MH * META].rearrange("p (h m) -> p h m", h=MH), AX.X, ALU.max)
                    S = ps[:, bank:bank + 2, :].rearrange("p a b -> p (a b)")
                    if t == LAST:
                        link(dve.memset(S[SAMPLE:R, 0:w], NEG))
                    else:
                        link(dve.memset(S[0:64, w - 64:w], NEG))
                    link(dve.tensor_reduce(sm_stat[0:R, 0, hd:hd + 1], S[0:R, 0:w], AX.X, ALU.max))
                    dve.tensor_scalar(nbias[0:R, i % 2, hd:hd + 1], sm_stat[0:R, 0, hd:hd + 1],
                                      sm_stat[0:R, 1, hd:hd + 1], -SCALE, ALU.max, ALU.mult).then_inc(s_nb, 1)
                if kind == "wo":
                    dve.wait_ge(s_sps2, k + 1)
                    dve.wait_ge(s_xres[i % 2], 32 * (i // 2 + 1))
                    h3 = h_row[0:R, i % 2, :].rearrange("p (a b) -> p a b", a=2)
                    dve.tensor_tensor(h3, h3, ps[0:R, bank:bank + 2, :], ALU.add).then_inc(rel, 1)
                if kind == "rt":
                    dve.wait_ge(s_sps2, k + 1)
                    dve.tensor_tensor(logits[0:R, t, :], ps[0:R, bank, 0:NG + NE], br_b[0:R, :],
                                      ALU.add).then_inc(rel, 1)
            if kind == "mpv":
                mrow = ps[0:R, 7, 0:MH * META].rearrange("p (h m) -> p h m", h=MH)
                dve.wait_ge(s_nb, (i + 1) * MH)
                dve.scalar_tensor_tensor(out=pm_row[0:R], in0=mrow, scalar=SCALE,
                                         in1=nbias[0:R, i % 2, :].unsqueeze(2).to_broadcast([R, MH, META]),
                                         op0=ALU.mult, op1=ALU.add).then_inc(s_dm, 1)
                dve.wait_ge(s_pm, i + 1)
                s_wait_read(dve, ("score", i, MH - 1))
                link(dve.tensor_reduce(sm_stat[0:R, 3, :], pm_row[0:R], AX.X, ALU.add))
                link(dve.tensor_tensor(sm_stat[0:R, 3, :], sm_stat[0:R, 3, :], sm_stat[0:R, 2, :], ALU.add))
                link(dve.reciprocal(sm_stat[0:R, 4, :], sm_stat[0:R, 3, :]))
                evacuate(dve, "dve", st)
                dve.wait_ge(s_pused, P_INDEX[st + (0,)] + 1)
                dve.tensor_tensor(mix_row[0:R, :].rearrange("p (h v) -> p h v", h=MH),
                                  ps[0:R, 6, :].rearrange("p (h v) -> p h v", h=MH),
                                  sm_stat[0:R, 4, :].unsqueeze(2).to_broadcast([R, MH, VD]), ALU.mult
                                  ).then_inc(s_mix, 1)
            if kind == "hn":
                dve.wait_ge(s_hrs, i + 1)
                dve.scalar_tensor_tensor(out=hn_row[0:R], in0=h_row[0:R, i % 2, :], scalar=h_stat[0:R, i % 2, 1:2],
                                         in1=fn_b[0:R, :], op0=ALU.mult, op1=ALU.mult).then_inc(s_hn, 1)

    s_rexp_in = sem("s_rexp_in")
    s_rexp = sem("s_rexp")
    s_cnt = sem("s_cnt")
    s_rank = sem("s_rank")
    s_slots = sem("s_slots")
    s_etab = sem("s_etab")
    s_tok0 = sem("s_tok0")
    s_tokz = sem("s_tokz")
    s_scat = sem("s_scat")
    s_tokr = sem("s_tokr")
    s_tokt = sem("s_tokt")
    s_toki = sem("s_toki")
    s_we = [sem(f"s_we{i}") for i in range(3)]
    s_xg = [sem(f"s_xg{i}") for i in range(3)]
    s_yst = [sem(f"s_yst{i}") for i in range(3)]
    s_mx = sem("s_mx")
    s_mxa = sem("s_mxa")
    s_mxv = sem("s_mxv")
    s_mh = sem("s_mh")
    s_ms = sem("s_ms")
    s_mg = sem("s_mg")
    s_mgt = sem("s_mgt")
    s_mgv = sem("s_mgv")
    s_my = sem("s_my")
    s_mya = sem("s_mya")
    s_myv = sem("s_myv")
    s_fin_w = sem("s_fin_w")
    s_res = [sem(f"s_res{i}") for i in range(2)]
    s_yab = [sem(f"s_yab{i}") for i in range(2)]
    s_comb = sem("s_comb")
    s_ysq = sem("s_ysq")
    s_yrs = sem("s_yrs")
    s_yo = sem("s_yo")
    s_yout = [sem(f"s_yout{i}") for i in range(2)]
    UN = 3
    TURNS = SLOT_TILES // UN
    assert SLOT_TILES % UN == 0

    def expert_turns(eng, body):
        for j in range(UN):
            body(0, j, True, False)
        with eng.Fori(1, TURNS - 1) as it:
            for j in range(UN):
                body(it, j, False, False)
        for j in range(UN):
            body(TURNS - 1, j, False, j == UN - 1)

    def moe_loads(sp):
        sp.wait_ge(s_tok0, 1)
        sp.dma_start(tok_dram.rearrange("(p s) o -> p (s o)", p=P), tok_rows[:, 0:SLOT_TILES]).then_inc(s_tokz, 16)
        sp.wait_ge(s_scat, 16 * 2 * NT)
        sp.dma_start(tok_rows[0:SLOT_TILES, :], tok_dram.rearrange("(s p) o -> s (p o)", p=P)).then_inc(s_tokr, 16)
        sp.wait_ge(s_etab, 1)

        def body(it, j, first, last):
            s = it * UN + j
            if not first:
                sp.wait_ge(s_my, s - UN + 1)
            e = sp.value_load(expert_of[0:1, bass.ds(s, 1)], min_val=0, max_val=NE - 1)
            sp.dma_start(w13_e[:, j, :, 0:FF],
                         w1[0, bass.ds(e, 1)].rearrange("e (c p) f -> p (e c) f", p=P)).then_inc(s_we[j], 16)
            sp.dma_start(w13_e[:, j, :, FF:2 * FF],
                         w3[0, bass.ds(e, 1)].rearrange("e (c p) f -> p (e c) f", p=P)).then_inc(s_we[j], 16)
            sp.dma_start(w2_e[:, j], w2[0, bass.ds(e, 1)].rearrange("e (c p) n -> p (e c) n", p=P)).then_inc(s_we[j], 16)
            if not first:
                store_y(s - UN)
                sp.dma_start(y_dram[bass.ds((s - UN) * P, P), :], y_row[:, j, :]).then_inc(s_yst[j], 16)

        def store_y(s):
            sp.wait_ge(s_mya, s + 1)
            sp.wait_ge(s_myv, s + 1)

        expert_turns(sp, body)
        for j in range(UN):
            s = SLOT_TILES - UN + j
            store_y(s)
            sp.dma_start(y_dram[s * P:(s + 1) * P, :], y_row[:, j, :]).then_inc(s_yst[j], 16)
        sp.wait_ge(phase_end, 16)
        sp.dma_start(fin_b, final_norm.rearrange("(a n) -> a n", a=1).to_broadcast([P, D])).then_inc(s_fin_w, 16)

        def load_res(t):
            R = ROWS[t]
            if t >= 2:
                sp.wait_ge(s_yo, t - 1)
            sp.dma_start(res[0:R, t % 2, :], h1_dram[t * P:t * P + R, :]).then_inc(s_res[t % 2], 16)

        sp.wait_ge(s_h1st, 16 * NT)
        load_res(0)
        load_res(1)
        for t in range(NT):
            R = ROWS[t]
            sp.wait_ge(s_yo, t + 1)
            if t < 8:
                sp.dma_start(y_prompt[0, t * P:(t + 1) * P, :], y_out[:, t % 2, :]).then_inc(s_yout[t % 2], 16)
            else:
                sp.dma_start(y_sample[0], y_out[0:SAMPLE, 0, :]).then_inc(s_yout[0], 16)
            if t + 2 < NT:
                load_res(t + 2)
        sp.wait_ge(s_yout[0], 16 * 5)
        sp.wait_ge(s_yout[1], 16 * 4)

    def moe_pool(pool, rsqrt_mean):
        pool.wait_ge(s_slots, 2)
        pool.wait_ge(s_tokz, 16)
        for t in range(NT):
            for k in range(2):
                pool.indirect_dma_start(
                    out=tok_dram, out_offset=bass.IndirectOffsetOnAxis(ap=slot_i[0:ROWS[t], k, t:t + 1], axis=0),
                    in_=tab[0:ROWS[t], C_TOK + t:C_TOK + t + 1], in_offset=None).then_inc(s_scat, 16)
        pool.wait_ge(s_toki, 1)
        pool.wait_ge(s_hnst, 16 * NT)
        for s in range(SLOT_TILES):
            if s >= UN:
                pool.wait_ge(s_mx, s - UN + 1)
            pool.indirect_dma_start(
                out=xg[:, s % UN, :], out_offset=None, in_=hn_dram,
                in_offset=bass.IndirectOffsetOnAxis(ap=tok_i[:, s:s + 1], axis=0)).then_inc(s_xg[s % UN], 16)
        end_phase(pool, 3)
        for j in range(UN):
            pool.wait_ge(s_yst[j], 16 * TURNS)

        def fetch(t):
            if t >= 2:
                pool.wait_ge(s_comb, t - 1)
            for k, dst in enumerate((ya, yb)):
                pool.indirect_dma_start(
                    out=dst[0:ROWS[t], t % 2, :], out_offset=None, in_=y_dram,
                    in_offset=bass.IndirectOffsetOnAxis(ap=slot_i[0:ROWS[t], k, t:t + 1], axis=0)
                    ).then_inc(s_yab[t % 2], 16)

        fetch(0)
        fetch(1)
        for t in range(NT):
            R = ROWS[t]
            rsqrt_mean(y_stat[0:R, 1, t:t + 1], y_stat[0:R, 0, t:t + 1], D, s_ysq, s_yrs, t + 1)
            if t + 2 < NT:
                fetch(t + 2)

    def moe_act(act):
        act.wait_ge(s_rexp_in, 1)
        act.activation(rt[:, 8, 0:45], rt[:, 8, 0:45], ACT.Exp).then_inc(s_rexp, 1)

        def turn_half(s):
            act.wait_ge(s_mx, s + 1)
            act.wait_ge(s_mh, s) if not isinstance(s, int) or s > 0 else None
            act.activation(xg_t[:, 0:4, :], ps[:, 0, :].rearrange("p (a b) -> p a b", a=4), ACT.Copy).then_inc(s_mxa, 1)

        def y_half(s, j):
            act.wait_ge(s_my, s + 1)
            return act.activation(y_row[:, j, 0:512], ps[:, 6, :], ACT.Copy).then_inc(s_mya, 1)

        turn_half(0)

        def body(it, j, first, last):
            s = it * UN + j
            start = first and j == 0
            act.wait_ge(s_mh, s + 1)
            if not start:
                act.wait_ge(s_mg, s)
            act.activation(act_h, ps[:, 3 + j, 0:FF], ACT.Silu).then_inc(s_ms, 1)
            if not start:
                pj = (j - 1) % UN
                if not first:
                    free_y(act, it, j)
                y_half(s - 1, pj)
            if not last:
                turn_half(s + 1)

        expert_turns(act, body)
        free_last(act)
        y_half(SLOT_TILES - 1, UN - 1)
        end_phase(act, 3)
        for t in range(NT):
            R = ROWS[t]
            act.wait_ge(s_comb, t + 1)
            if t:
                act.wait_ge(s_ysq, t)
            act.activation(y_sq[0:R], res[0:R, t % 2, :], ACT.Square,
                           accum_out=y_stat[0:R, 0, t:t + 1]).then_inc(s_ysq, 1)

    def free_y(eng, it, j):
        pj = (j - 1) % UN
        if j == 0:
            if isinstance(it, int) and it < 2:
                return
            n = it - 1
        else:
            n = it
        eng.wait_ge(s_yst[pj], n * 16)

    def free_last(eng):
        eng.wait_ge(s_yst[UN - 1], (TURNS - 1) * 16)

    def moe_pe(pe):
        pe.wait_ge(s_cnt, 1)
        pe.matmul(ps[:, 0, 0:NT * NE], tab[:, C_TRI:C_TRI + P], rt[:, 15, :], start=True, stop=True)
        pe.matmul(ps[:, 1, 0:NT * NE], ones, rt[:, 15, :], start=True, stop=True).then_inc(s_rank, 1)
        pe.wait_ge(s_tokr, 16)
        pe.transpose(ps[:, 2, 0:SLOT_TILES], tok_rows[0:SLOT_TILES, :],
                     ident[0:SLOT_TILES, 0:SLOT_TILES]).then_inc(s_tokt, 1)

        def turn(s, it, j):
            pe.wait_ge(s_xg[j], 16 * (it + 1) if not isinstance(it, int) else 16 * (it + 1))
            if not (isinstance(s, int) and s == 0):
                pe.wait_ge(s_mxa, s)
                pe.wait_ge(s_mxv, s)
            for kc in range(KC):
                ins = pe.transpose(ps[:, kc // 4, (kc % 4) * P:(kc % 4 + 1) * P], xg[:, j, kc * P:(kc + 1) * P], ident)
            ins.then_inc(s_mx, 1)

        def down(s, j):
            pe.wait_ge(s_mgv, s + 1)
            if not (isinstance(s, int) and s == 0):
                pe.wait_ge(s_mya, s)
                pe.wait_ge(s_myv, s)
            for n in range(2):
                for c in range(2):
                    ins = pe.matmul(ps[:, 6 + n, :], g_t[:, c, :], w2_e[:, j, c, n * 512:(n + 1) * 512],
                                    start=c == 0, stop=c == 1)
            ins.then_inc(s_my, 1)

        pe.wait_ge(s_toki, 1)
        turn(0, 0, 0)

        def body(it, j, first, last):
            s = it * UN + j
            start = first and j == 0
            pe.wait_ge(s_mxa, s + 1)
            pe.wait_ge(s_mxv, s + 1)
            pe.wait_ge(s_we[j], (it + 1) * 48)
            if not first:
                pe.wait_ge(s_mg, s - UN + 1)
            for kc in range(KC):
                ins = pe.matmul(ps[:, 3 + j, :], xg_t[:, kc, :], w13_e[:, j, kc, :], start=kc == 0, stop=kc == KC - 1)
            ins.then_inc(s_mh, 1)
            if not start:
                down(s - 1, (j - 1) % UN)
            if not last:
                turn(s + 1, it + (j + 1) // UN, (j + 1) % UN)
            pe.wait_ge(s_mg, s + 1)
            if not start:
                pe.wait_ge(s_mgv, s)
            for c in range(2):
                ins = pe.transpose(ps[:, 2, c * P:(c + 1) * P], g_row[:, c * P:(c + 1) * P], ident)
            ins.then_inc(s_mgt, 1)

        expert_turns(pe, body)
        down(SLOT_TILES - 1, UN - 1)
        end_phase(pe, 3)

    def moe_dve(dve, link):
        row = lambda k: rt[:, k, :]
        v9 = lambda k, n: rt[:, k, 0:NT * n].rearrange("p (t n) -> p t n", t=NT)
        col = lambda k: rt[:, k, 0:NT]
        w4 = tab[:, C_W4:C_W4 + 4].unsqueeze(1).to_broadcast([P, NT, 4])
        dve.memset(tok_rows, 0.0).then_inc(s_tok0, 1)

        def bc(x, n):
            return x.unsqueeze(2).to_broadcast([P, NT, n])

        def first_max(x, m, oh, tmp, tmp1):
            link(dve.tensor_reduce(m, x, AX.X, ALU.max))
            link(dve.tensor_tensor(tmp, x, bc(m, 4), ALU.is_equal))
            link(dve.tensor_tensor(tmp, tmp, w4, ALU.mult))
            link(dve.tensor_reduce(tmp1, tmp, AX.X, ALU.max))
            link(dve.tensor_tensor(oh, tmp, bc(tmp1, 4), ALU.is_equal))

        lg = logits[:, :, 0:NG]
        le = logits[:, :, NG:]
        oh_g, oh_1, oh_2, tmp, sel = v9(0, 4), v9(1, 4), v9(2, 4), v9(3, 4), v9(4, 4)
        m_g, m_1, m_2, t1 = col(5), col(6), col(7), col(9)
        first_max(lg, m_g, oh_g, tmp, t1)
        t16 = rt[:, 10, :].rearrange("p (t g j) -> p t g j", t=NT, g=NG)
        link(dve.tensor_tensor(t16, le.rearrange("p t (g j) -> p t g j", g=NG),
                               oh_g.unsqueeze(3).to_broadcast([P, NT, NG, EG]), ALU.mult))
        link(dve.tensor_reduce(sel, t16.rearrange("p t g j -> p t j g"), AX.X, ALU.add))
        first_max(sel, m_1, oh_1, tmp, t1)
        link(dve.scalar_tensor_tensor(out=sel, in0=oh_1, scalar=-3e38, in1=sel, op0=ALU.mult, op1=ALU.add))
        first_max(sel, m_2, oh_2, tmp, t1)
        link(dve.tensor_tensor(rt[:, 8, 0:36].rearrange("p (t n) -> p t n", t=NT), lg, bc(m_g, 4), ALU.subtract))
        dve.tensor_tensor(rt[:, 8, 36:45], m_2, m_1, ALU.subtract).then_inc(s_rexp_in, 1)
        valid = bc(tab[:, C_VALID:C_VALID + NT], NE)
        for k, oh in ((13, oh_1), (14, oh_2)):
            link(dve.tensor_tensor(rt[:, k, :].rearrange("p (t g j) -> p t g j", t=NT, g=NG),
                                   oh_g.unsqueeze(3).to_broadcast([P, NT, NG, EG]),
                                   oh.unsqueeze(2).to_broadcast([P, NT, NG, EG]), ALU.mult))
            link(dve.tensor_tensor(v9(k, NE), v9(k, NE), valid, ALU.mult))
        dve.tensor_tensor(row(15), row(13), row(14), ALU.add).then_inc(s_cnt, 1)
        dve.wait_ge(s_rexp, 1)
        link(dve.tensor_reduce(t1, rt[:, 8, 0:36].rearrange("p (t n) -> p t n", t=NT), AX.X, ALU.add))
        link(dve.reciprocal(t1, t1))
        link(dve.tensor_scalar(col(11), rt[:, 8, 36:45], 1.0, None, ALU.add))
        link(dve.reciprocal(col(11), col(11)))
        link(dve.tensor_tensor(gates[:, 0, :], t1, col(11), ALU.mult))
        link(dve.tensor_tensor(gates[:, 1, :], gates[:, 0, :], rt[:, 8, 36:45], ALU.mult))
        dve.wait_ge(s_rank, 1)
        base = v9(16, NE)
        link(dve.memset(base[:, 0, :], 0.0))
        for t in range(NT - 1):
            link(dve.tensor_tensor(base[:, t + 1, :], base[:, t, :], ps[:, 1, t * NE:(t + 1) * NE], ALU.add))
        count, tiles, incl, offs, zero = (rt[:, 17, k * NE:(k + 1) * NE] for k in range(5))
        link(dve.tensor_tensor(count, base[:, NT - 1, :], ps[:, 1, (NT - 1) * NE:NT * NE], ALU.add))
        link(dve.memset(zero, 0.0))
        over = rt[:, 18, :].rearrange("p (e k) -> p e k", e=NE)
        link(dve.tensor_tensor(over, count.unsqueeze(2).to_broadcast([P, NE, 9]),
                               tab[:, C_THR:C_THR + 9].unsqueeze(1).to_broadcast([P, NE, 9]), ALU.is_gt))
        link(dve.tensor_reduce(tiles, over, AX.X, ALU.add))
        link(dve.tensor_tensor_scan(incl, tiles, zero, 0.0, ALU.add, ALU.add))
        link(dve.tensor_tensor(offs, incl, tiles, ALU.subtract))
        link(dve.tensor_scalar(offs, offs, float(P), None, ALU.mult))
        link(dve.tensor_tensor(row(16), row(16), ps[:, 0, 0:NT * NE], ALU.add))
        link(dve.tensor_tensor(v9(16, NE), v9(16, NE), offs.unsqueeze(1).to_broadcast([P, NT, NE]), ALU.add))
        for k in range(2):
            link(dve.tensor_tensor(row(13 + k), row(13 + k), row(16), ALU.mult))
            link(dve.tensor_reduce(t1, v9(13 + k, NE), AX.X, ALU.add))
            dve.tensor_copy(slot_i[:, k, :], t1).then_inc(s_slots, 1)
            dve.wait_ge(s_slots, k + 1)
        le_tab = rt[:, 19:23, :].rearrange("p a b -> p (a b)")[:, 0:SLOT_TILES * NE].rearrange(
            "p (s e) -> p s e", s=SLOT_TILES)
        link(dve.tensor_tensor(le_tab, incl.unsqueeze(1).to_broadcast([P, SLOT_TILES, NE]),
                               tab[:, C_IOTA:C_IOTA + SLOT_TILES].unsqueeze(2).to_broadcast([P, SLOT_TILES, NE]),
                               ALU.is_le))
        link(dve.tensor_reduce(rt[:, 23, 0:SLOT_TILES], le_tab, AX.X, ALU.add))
        link(dve.tensor_scalar(rt[:, 23, 0:SLOT_TILES], rt[:, 23, 0:SLOT_TILES], float(NE - 1), None, ALU.min))
        dve.tensor_copy(expert_of, rt[:, 23, 0:SLOT_TILES]).then_inc(s_etab, 1)
        dve.wait_ge(s_tokt, 1)
        dve.tensor_copy(tok_i, ps[:, 2, 0:SLOT_TILES]).then_inc(s_toki, 1)

        def turn_half(s):
            dve.wait_ge(s_mx, s + 1)
            if not (isinstance(s, int) and s == 0):
                dve.wait_ge(s_mh, s)
            dve.tensor_copy(xg_t[:, 4:8, :], ps[:, 1, :].rearrange("p (a b) -> p a b", a=4)).then_inc(s_mxv, 1)

        def y_half(s, j):
            dve.wait_ge(s_my, s + 1)
            dve.tensor_copy(y_row[:, j, 512:1024], ps[:, 7, :]).then_inc(s_myv, 1)

        turn_half(0)

        def body(it, j, first, last):
            s = it * UN + j
            start = first and j == 0
            dve.wait_ge(s_ms, s + 1)
            if not start:
                dve.wait_ge(s_mgt, s)
            dve.tensor_tensor(g_row, act_h, ps[:, 3 + j, FF:2 * FF], ALU.mult).then_inc(s_mg, 1)
            if not start:
                if not first:
                    free_y(dve, it, j)
                y_half(s - 1, (j - 1) % UN)
            if not last:
                turn_half(s + 1)
            dve.wait_ge(s_mgt, s + 1)
            if not start:
                dve.wait_ge(s_my, s)
            dve.tensor_copy(g_t, ps[:, 2, 0:2 * P].rearrange("p (a b) -> p a b", a=2)).then_inc(s_mgv, 1)

        expert_turns(dve, body)
        free_last(dve)
        y_half(SLOT_TILES - 1, UN - 1)
        end_phase(dve, 3)
        dve.wait_ge(s_fin_w, 16)

        def finish(t):
            R = ROWS[t]
            dve.wait_ge(s_yrs, t + 1)
            if t >= 2:
                dve.wait_ge(s_yout[t % 2], 16 * (t // 2))
            dve.scalar_tensor_tensor(out=y_out[0:R, t % 2, :], in0=res[0:R, t % 2, :], scalar=y_stat[0:R, 1, t:t + 1],
                                     in1=fin_b[0:R, :], op0=ALU.mult, op1=ALU.mult).then_inc(s_yo, 1)

        for t in range(NT):
            R = ROWS[t]
            dve.wait_ge(s_res[t % 2], 16 * (t // 2 + 1))
            dve.wait_ge(s_yab[t % 2], 32 * (t // 2 + 1))
            x = res[0:R, t % 2, :]
            link(dve.scalar_tensor_tensor(out=x, in0=ya[0:R, t % 2, :], scalar=gates[0:R, 0, t:t + 1], in1=x,
                                          op0=ALU.mult, op1=ALU.add))
            dve.scalar_tensor_tensor(out=x, in0=yb[0:R, t % 2, :], scalar=gates[0:R, 1, t:t + 1], in1=x,
                                     op0=ALU.mult, op1=ALU.add).then_inc(s_comb, 1)
            if t:
                finish(t - 1)
        finish(NT - 1)

    N_OUT = 2

    blk = ctx.enter_context(nc.Block())

    @blk.sync
    def _(sp):
        sp.dma_start(tab, table).then_inc(s_tab, 16)
        sp.dma_start(masks, level_masks).then_inc(s_tab, 16)
        sp.dma_start(an_b, attn_norm[0:1, :].to_broadcast([P, D])).then_inc(s_norm_w, 16)

        def load_x(t):
            if t >= 2:
                sp.wait_ge(s_xs, t - 1)
            if t < 8:
                sp.dma_start(x_row[:, t % 2, :], x_prompt[0, t * P:(t + 1) * P, :]).then_inc(s_xrow[t % 2], 32)
            else:
                sp.dma_start(x_row[0:SAMPLE, 0, :], x_sample[0]).then_inc(s_xrow[0], 16)
                sp.dma_start(x_row[SAMPLE:SAMPLE + META, 0, :], meta_tokens).then_inc(s_xrow[0], 16)

        def load_w(g):
            _, a, n = GROUPS[g]
            if g >= 2:
                sp.wait_ge(s_zps, sum(1 for z in Z_OUT if z[1] <= g - 2))
            sp.dma_start(w_grp[:, g % 2, :, 0:n],
                         w_in[0].rearrange("(c p) n -> p c n", p=P)[:, :, a:a + n]).then_inc(s_wg[g % 2], 16)

        load_x(0)
        load_x(1)
        load_w(0)
        load_w(1)
        for r_ in range(2):
            sp.dma_start(lbl[:, r_, :], hg_lb_logits[r_].rearrange("(h k) -> k h", k=HK),
                         allow_slow_non_contiguous=True).then_inc(s_hin, 16)
        sp.dma_start(gn_b, hg_gnorm[0:1, :].to_broadcast([P, HK])).then_inc(s_hin, 16)
        for t in range(2, NT):
            load_x(t)
        for g in range(2, len(GROUPS)):
            load_w(g)
        sp.wait_ge(phase_end, 4)
        sp.dma_start(state_s, state_hgrn[0, 0].rearrange("h k v -> k h v")).then_inc(s_st0, 16)
        sp.wait_ge(s_sev, 2)
        sp.dma_start(hgrn_sample[0, 0].rearrange("h k v -> k h v"), state_s).then_inc(s_out, 16)
        sp.wait_ge(s_sev, NT + 1)
        sp.dma_start(hgrn_prompt[0, 0].rearrange("h k v -> k h v"), state).then_inc(s_out, 16)
        attention_loads(sp)
        moe_loads(sp)
        sp.wait_ge(s_out, 16 * N_OUT)

    @blk.gpsimd
    def _(pool):
        def rsqrt_mean(out, ssq, n, before, after, count):
            pool.wait_ge(before, count)
            pool.tensor_scalar(out, ssq, 1.0 / n, EPS, ALU.mult, ALU.add).then_inc(s_pool, 1)
            pool_chain[0] += 1
            pool.wait_ge(s_pool, pool_chain[0])
            return pool.tensor_tensor(out, out, neg_half[0:out.shape[0], 0:out.shape[1]], ALU.pow).then_inc(after, 1)

        for n, (what, value) in enumerate([(z_mla[64:P, LAST, :], 0.0), (v_hg[64:P, LAST, :], 0.0),
                                           (hg_out[64:P, LAST, :], 0.0), (q_hg[:, :, T:TP], 0.0),
                                           (f_hg[:, :, T:TP], 1.0), (logits[64:P, LAST, :], 0.0)]):
            pool.memset(what, value).then_inc(s_zero, 1)
            pool.wait_ge(s_zero, n + 1)
        pool.wait_ge(s_tab, 32)
        for t in range(NT):
            rsqrt_mean(stat[0:ROWS[t], 16 + t:17 + t], stat[0:ROWS[t], t:t + 1], D, s_ssq, s_rstd, t + 1)
        pool.wait_ge(s_hin, 48)
        for t in range(NT):
            pool.wait_ge(s_zev, 2 * NT + t + 1)
            w = hg_out[:, t, :].rearrange("p (h v) -> p h v", h=HH)
            pool.tensor_tensor(w, w, gn_b.unsqueeze(1).to_broadcast([P, HH, HK]), ALU.mult).then_inc(s_gs, 1)
        end_phase(pool, 0)
        for i, c in enumerate(ORDER):
            rsqrt_mean(o_rstd[0:ROWS[c], i % 2, :], o_stat[0:ROWS[c], i % 2, :], HK, s_osq, s_ors, i + 1)
        end_phase(pool, 1)
        attention_pool(pool, rsqrt_mean)
        end_phase(pool, 2)
        moe_pool(pool, rsqrt_mean)

    @blk.scalar
    def _(act):
        act.wait_ge(s_tab, 32)
        for t in range(NT):
            act.wait_ge(s_xrow[t % 2], 32 * (t // 2 + 1))
            if t:
                act.wait_ge(s_ssq, t)
            act.activation(ps[0:ROWS[t], 0:2, :], x_row[0:ROWS[t], t % 2, :].rearrange("p (a b) -> p a b", a=2),
                           ACT.Square, accum_out=stat[0:ROWS[t], t:t + 1]).then_inc(s_ssq, 1)
            if t >= 1:
                x_half(act, t - 1)
        x_half(act, NT - 1)
        act.wait_ge(s_zero, 6)
        for n, (kind, g, m, k) in enumerate(Z_OUT):
            act.wait_ge(s_zps, n + 1)
            bank = n % Z_RING
            if kind == "mla":
                act.activation(z_mla[0:ROWS[m], m, :], ps[0:ROWS[m], bank, 0:ZA], ACT.Copy).then_inc(s_zev, 1)
            elif kind == "v":
                act.activation(v_hg[0:ROWS[m], m, :], ps[0:ROWS[m], bank, :], ACT.Copy).then_inc(s_zev, 1)
            elif kind == "gate":
                act.activation(hg_out[0:ROWS[m], m, :], ps[0:ROWS[m], bank, :], ACT.Silu).then_inc(s_zev, 1)
            elif kind == "f":
                act.activation(f_hg[:, m, k * ZN:(k + 1) * ZN], ps[:, bank, 0:ZN], ACT.Sigmoid).then_inc(s_zev, 1)
            else:
                act.activation(q_hg[:, m, k * ZN:(k + 1) * ZN], ps[:, bank, 0:ZN], ACT.Silu).then_inc(s_zev, 1)
        act.wait_ge(s_lb, 3)
        act.activation(lb[:, 0:2, :], lb[:, 0:2, :], ACT.Exp).then_inc(s_lbe, 1)
        end_phase(act, 0)
        for i, c in enumerate(ORDER):
            lv = levels(c)
            for n, h in enumerate(lv):
                k = LV0[i] + n
                nxt, cur = (k + 1) % 3, k % 3
                act.wait_ge(s_lvl, 2 * k + 2 * i + 2)
                if k >= 1:
                    act.wait_ge(s_cpy, 2 * k)
                if n >= 2:
                    act.wait_ge(s_prod, PR0[i] + n)
                a = q_lv[:, nxt].rearrange("p h (b u w) -> p h b u w", u=2, w=h)
                b = q_lv[:, cur].rearrange("p h (b u w) -> p h b u w", u=2, w=h)
                act.activation(a[:, :, :, 0, :], b[:, :, :, 0, :], ACT.Copy).then_inc(s_cpy, 1)
                a = k_lv[:, nxt].rearrange("p h (b u w) -> p h b u w", u=2, w=h)
                b = k_lv[:, cur].rearrange("p h (b u w) -> p h b u w", u=2, w=h)
                act.activation(a[:, :, :, 1, :], b[:, :, :, 1, :], ACT.Copy).then_inc(s_cpy, 1)
            act.wait_ge(s_ktp, i + 1)
            if i >= 1:
                act.wait_ge(s_sps, i)
            act.activation(k_rows, ps[:, 4, :].rearrange("p (h k) -> p h k", h=HH), ACT.Copy).then_inc(s_kte, 1)
            act.wait_ge(s_ops, i + 1)
            for hd in range(HH):
                ins = act.activation(ps[0:ROWS[c], 6, hd * P:(hd + 1) * P], ps[0:ROWS[c], 3, hd * P:(hd + 1) * P],
                                     ACT.Square, accum_out=o_stat[0:ROWS[c], i % 2, hd:hd + 1])
            ins.then_inc(s_osq, 1)
        end_phase(act, 1)
        attention_act(act)
        end_phase(act, 2)
        moe_act(act)

    @blk.tensor
    def _(pe):
        pe.wait_ge(s_tab, 32)
        for t in range(NT):
            pe.wait_ge(s_xs, t + 1)
            for half in range(2):
                if t:
                    pe.wait_ge(s_xta if half == 0 else s_xtv, t)
                for k in range(4):
                    kc = 4 * half + k
                    ins = pe.transpose(ps[:, 6 + half, k * P:k * P + ROWS[t]], xs[0:ROWS[t], 0, kc * P:(kc + 1) * P],
                                       ident[0:ROWS[t], 0:ROWS[t]])
                ins.then_inc(s_xps, 1)
        pe.wait_ge(s_xta, NT)
        pe.wait_ge(s_xtv, NT)
        for n, (kind, g, m, k) in enumerate(Z_OUT):
            if n == 0 or Z_OUT[n - 1][1] != g:
                pe.wait_ge(s_wg[g % 2], 16 * (g // 2 + 1))
            if n >= Z_RING:
                pe.wait_ge(s_zev, n - Z_RING + 1)
            w = w_grp[:, g % 2]
            bank = n % Z_RING
            for kc in range(KC):
                if kind in ("f", "q"):
                    ins = pe.matmul(ps[:, bank, 0:ZN], w[:, kc, m * P:(m + 1) * P], x_t[:, kc, k * ZN:(k + 1) * ZN],
                                    start=kc == 0, stop=kc == KC - 1)
                else:
                    nn = GROUPS[g][2]
                    ins = pe.matmul(ps[0:ROWS[m], bank, 0:nn], x_t[:, kc, col0(m):col0(m) + ROWS[m]], w[:, kc, 0:nn],
                                    start=kc == 0, stop=kc == KC - 1)
            ins.then_inc(s_zps, 1)
        end_phase(pe, 0)
        pe.wait_ge(s_st0, 16)
        for i, c in enumerate(ORDER):
            lv = levels(c)
            cs = slice(col0(c), col0(c) + P)
            for n in range(len(lv) + 1):
                pr = PR0[i] + n
                bank = pr % 3
                if pr >= 3:
                    pe.wait_ge(s_mask, pr - 2)
                if n == 0:
                    for hd in range(HH):
                        ins = pe.matmul(ps[:, bank, hd * P:(hd + 1) * P], k_hg[:, hd, cs], q_hg[:, hd, cs],
                                        start=True, stop=True)
                else:
                    h = lv[n - 1]
                    k = LV0[i] + n - 1
                    pe.wait_ge(s_lvl, 2 * k + 2 * i + 2)
                    if k:
                        pe.wait_ge(s_cpy, 2 * k)
                    for hd in range(HH):
                        tq = q_lv[:, k % 3, hd, :].rearrange("p (b u w) -> p b u w", u=2, w=h)[:, :, 1, :]
                        ins = pe.matmul(ps[:, bank, hd * 64:(hd + 1) * 64], k_lv[:, k % 3, hd, :], tq,
                                        start=True, stop=True)
                ins.then_inc(s_prod, 1)
            fin = (LV0[i] + len(lv)) % 3
            pe.wait_ge(s_lvl, 2 * LV0[i + 1] + 2 * i + 2)
            pe.wait_ge(s_cpy, 2 * LV0[i + 1])
            if i:
                pe.wait_ge(s_kte, i)
            for hd in range(HH):
                ins = pe.transpose(ps[:, 4, hd * P:(hd + 1) * P], k_lv[:, fin, hd, :], ident)
            ins.then_inc(s_ktp, 1)
            pe.wait_ge(s_mask, PR0[i + 1])
            if i:
                pe.wait_ge(s_oev, i)
                pe.wait_ge(s_sev, i + 1)
            R = ROWS[c]
            for hd in range(HH):
                o = ps[:, 3, hd * P:(hd + 1) * P]
                pe.matmul(o[0:R], attn_t[0:R, i % 2, hd, 0:R], v_hg[0:R, c, hd * P:(hd + 1) * P],
                          start=hd == 0, stop=False, skip_group_check=True)
                if c == LAST:
                    ins = pe.matmul(o[0:SAMPLE], q_lv[:, fin, hd, 0:SAMPLE], state_s[:, hd, :],
                                    start=False, stop=True, skip_group_check=True)
                else:
                    ins = pe.matmul(o[0:R], q_lv[:, fin, hd, :], state[:, hd, :],
                                    start=False, stop=True, skip_group_check=True)
            ins.then_inc(s_ops, 1)
            pe.wait_ge(s_kte, i + 1)
            for hd in range(HH):
                vv = v_hg[:, c, hd * P:(hd + 1) * P]
                if c == LAST:
                    pe.matmul(ps[:, 5, hd * P:(hd + 1) * P], k_rows[0:SAMPLE, hd, :], vv[0:SAMPLE],
                              start=True, stop=True)
                    ins = pe.matmul(ps[:, 7, hd * P:(hd + 1) * P], k_rows[SAMPLE:SAMPLE + META, hd, :],
                                    vv[SAMPLE:SAMPLE + META], start=True, stop=True)
                else:
                    ins = pe.matmul(ps[:, 5, hd * P:(hd + 1) * P], k_rows[:, hd, :], vv, start=True, stop=True)
            ins.then_inc(s_sps, 1)
        end_phase(pe, 1)
        attention_pe(pe)
        end_phase(pe, 2)
        moe_pe(pe)

    @blk.vector
    def _(dve):
        def link(ins):
            dve_chain[0] += 1
            ins.then_inc(s_dve, 1)
            dve.wait_ge(s_dve, dve_chain[0])

        dve.wait_ge(s_norm_w, 16)

        def second_half(t):
            dve.wait_ge(s_xps, 2 * t + 2)
            dve.tensor_copy(x_t[:, 4:8, col0(t):col0(t) + ROWS[t]],
                            ps[:, 7, :].rearrange("p (a b) -> p a b", a=4)[:, :, 0:ROWS[t]]).then_inc(s_xtv, 1)

        for t in range(NT):
            dve.wait_ge(s_rstd, t + 1)
            dve.wait_ge(s_xrow[t % 2], 32 * (t // 2 + 1))
            if t:
                dve.wait_ge(s_xps, 2 * t)
            R = ROWS[t]
            dve.scalar_tensor_tensor(out=xs[0:R, 0, :], in0=x_row[0:R, t % 2, :], scalar=stat[0:R, 16 + t:17 + t],
                                     in1=an_b[0:R, :], op0=ALU.mult, op1=ALU.mult).then_inc(s_xs, 1)
            second_half(t)
        dve.wait_ge(s_hin, 48)
        dve.tensor_tensor(lb[:, 2, :], lbl[:, 0, :], lbl[:, 1, :], ALU.max).then_inc(s_lb, 1)
        dve.wait_ge(s_lb, 1)
        dve.tensor_tensor(lb[:, 0, :], lbl[:, 0, :], lb[:, 2, :], ALU.subtract).then_inc(s_lb, 1)
        dve.tensor_tensor(lb[:, 1, :], lbl[:, 1, :], lb[:, 2, :], ALU.subtract).then_inc(s_lb, 1)
        dve.wait_ge(s_lbe, 1)
        link(dve.tensor_tensor(lb[:, 2, :], lb[:, 0, :], lb[:, 1, :], ALU.add))
        link(dve.reciprocal(lb[:, 2, :], lb[:, 2, :]))
        link(dve.tensor_tensor(lb[:, 0, :], lb[:, 0, :], lb[:, 2, :], ALU.mult))
        link(dve.tensor_scalar(lb[:, 1, :], lb[:, 0, :], -1.0, 1.0, ALU.mult, ALU.add))
        for hd in range(HH):
            link(dve.tensor_scalar(f_hg[:, hd, 0:T], f_hg[:, hd, 0:T], lb[:, 1, hd:hd + 1], lb[:, 0, hd:hd + 1],
                                   ALU.mult, ALU.add))
            dve.tensor_scalar(k_hg[:, hd, :], f_hg[:, hd, :], -1.0, 1.0, ALU.mult, ALU.add).then_inc(s_fk, 1)
        end_phase(dve, 0)
        link(dve.memset(state, 0.0))
        dve.wait_ge(s_st0, 16)
        for i, c in enumerate(ORDER):
            lv = levels(c)
            cs = slice(col0(c), col0(c) + P)
            R = ROWS[c]
            k0 = LV0[i]
            if i:
                dve.wait_ge(s_prod, PR0[i])
                dve.wait_ge(s_ops, i)
                dve.wait_ge(s_ktp, i)
            dve.scalar_tensor_tensor(out=q_lv[:, k0 % 3], in0=q_hg[:, :, cs], scalar=QSCALE, in1=f_hg[:, :, cs],
                                     op0=ALU.mult, op1=ALU.mult).then_inc(s_lvl, 1)
            dve.tensor_copy(k_lv[:, k0 % 3], k_hg[:, :, cs]).then_inc(s_lvl, 1)
            dve.wait_ge(s_prod, PR0[i] + 1)
            if i >= 2:
                dve.wait_ge(s_ops, i - 1)
            dve.tensor_tensor(attn_t[:, i % 2], ps[:, PR0[i] % 3, :].rearrange("p (h t) -> p h t", h=HH),
                                   ident_q.unsqueeze(1).to_broadcast([P, HH, P]), ALU.mult).then_inc(s_mask, 1)
            dve.wait_ge(s_mask, PR0[i] + 1)
            src_tot = f_hg[:, :, cs]
            for n, h in enumerate(lv):
                k = k0 + n
                nxt, cur = (k + 1) % 3, k % 3
                nb = P // (2 * h)
                pair = src_tot.rearrange("p h (b u) -> p h b u", u=2)
                dve.wait_ge(s_lvl, 2 * k + 2 * i + 2)
                if k:
                    dve.wait_ge(s_cpy, 2 * k)
                if n >= 2:
                    dve.wait_ge(s_prod, PR0[i] + n)
                a = q_lv[:, nxt].rearrange("p h (b u w) -> p h b u w", u=2, w=h)
                b = q_lv[:, cur].rearrange("p h (b u w) -> p h b u w", u=2, w=h)
                dve.tensor_tensor(a[:, :, :, 1, :], b[:, :, :, 1, :],
                                  pair[:, :, :, 0].unsqueeze(3).to_broadcast([P, HH, nb, h]),
                                  ALU.mult).then_inc(s_lvl, 1)
                a = k_lv[:, nxt].rearrange("p h (b u w) -> p h b u w", u=2, w=h)
                b = k_lv[:, cur].rearrange("p h (b u w) -> p h b u w", u=2, w=h)
                dve.tensor_tensor(a[:, :, :, 0, :], b[:, :, :, 0, :],
                                  pair[:, :, :, 1].unsqueeze(3).to_broadcast([P, HH, nb, h]),
                                  ALU.mult).then_inc(s_lvl, 1)
                nt = tot[:, n, :, 0:nb]
                link(dve.tensor_tensor(nt, pair[:, :, :, 0], pair[:, :, :, 1], ALU.mult))
                src_tot = nt
                pr = PR0[i] + n + 1
                dve.wait_ge(s_prod, pr + 1)
                out = attn_t[:, i % 2].rearrange("p h (b u w) -> p h b u w", u=2, w=h)
                for hd in range(HH):
                    ins = dve.copy_predicated(
                        out[:, hd, :, 1, :],
                        masks[:, n * 64:(n + 1) * 64].rearrange("p (b w) -> p b w", w=h),
                        ps[:, pr % 3, hd * 64:(hd + 1) * 64].rearrange("p (b w) -> p b w", w=h))
                ins.then_inc(s_mask, 1)
                
            dve.wait_ge(s_sps, i + 1)
            if c == LAST:
                dve.wait_ge(s_ops, i + 1)
                for hd in range(HH):
                    ins = dve.scalar_tensor_tensor(out=state_s[:, hd, :], in0=state_s[:, hd, :],
                                                   scalar=src_tot[:, hd, 0:1],
                                                   in1=ps[:, 5, hd * P:(hd + 1) * P], op0=ALU.mult, op1=ALU.add)
                ins.then_inc(s_sev, 1)
                dve.tensor_copy(state, ps[:, 7, :].rearrange("p (h v) -> p h v", h=HH)).then_inc(s_sev, 1)
            else:
                dve.wait_ge(s_ops, i + 1)
                for hd in range(HH):
                    ins = dve.scalar_tensor_tensor(out=state[:, hd, :], in0=state[:, hd, :],
                                                   scalar=src_tot[:, hd, 0:1],
                                                   in1=ps[:, 5, hd * P:(hd + 1) * P], op0=ALU.mult, op1=ALU.add)
                ins.then_inc(s_sev, 1)
            dve.wait_ge(s_ors, i + 1)
            dve.wait_ge(s_gs, NT)
            for hd in range(HH):
                g_ = hg_out[0:R, c, hd * P:(hd + 1) * P]
                ins = dve.scalar_tensor_tensor(out=g_, in0=ps[0:R, 3, hd * P:(hd + 1) * P],
                                               scalar=o_rstd[0:R, i % 2, hd:hd + 1], in1=g_,
                                               op0=ALU.mult, op1=ALU.mult)
            ins.then_inc(s_oev, 1)
        end_phase(dve, 1)
        attention_dve(dve, link)
        end_phase(dve, 2)
        moe_dve(dve, link)

    ctx.close()


_INS = ["x_prompt", "x_sample", "cache_ckv", "cache_krope", "state_hgrn", "meta_tokens", "attn_norm", "w_in", "q_norm",
        "kv_norm", "w_uq", "w_uk", "w_uv", "hg_lb_logits", "hg_gnorm", "w_o", "ffn_norm", "w_router_group",
        "b_router_group", "w_router_expert", "b_router_expert", "w1", "w3", "w2", "final_norm"]
_OUTS = [(1, 1024, D), (1, SAMPLE, D), (1, 1, 1024 + META, CR), (1, 1, 1024 + META, RD), (1, 1, HH, HK, HK),
         (1, 1, SAMPLE, CR), (1, 1, SAMPLE, RD), (1, 1, HH, HK, HK)]


def kernel(**inputs):
    import numpy as np
    import concourse.bacc as bacc
    from concourse.bass_utils import run_bass_kernel_spmd

    nc = bacc.Bacc("TRN2", target_bir_lowering=False, num_devices=1)
    table, level_masks = constants()
    arrays, args = {}, []
    for name, a in [(n, np.ascontiguousarray(inputs[n])) for n in _INS] + [("table", table), ("masks", level_masks)]:
        arrays[f"in_{name}"] = a
        args.append(nc.dram_tensor(f"in_{name}", a.shape, mybir.dt.from_np(a.dtype), kind="ExternalInput").ap())
    for i, shape in enumerate(_OUTS):
        args.append(nc.dram_tensor(f"out_{i}", shape, F32, kind="ExternalOutput").ap())
    hybrid_layer(nc, *args)
    r = run_bass_kernel_spmd(nc, [arrays], core_ids=[0])
    return tuple(r.results[0][f"out_{i}"] for i in range(len(_OUTS)))
```

```python
from contextlib import ExitStack

import concourse.bass as bass
from concourse import mybir

F32 = mybir.dt.float32
F32R = mybir.dt.float32r
I32 = mybir.dt.int32
ALU = mybir.AluOpType
ACT = mybir.ActivationFunctionType
AX = mybir.AxisListType

P = 128
D = 1024
KC = D // P
NT = 9
LAST = 8
SAMPLE, META = 64, 16
ROWS = [P] * 8 + [SAMPLE + META]
T = 8 * P + SAMPLE + META
TP = NT * P
ORDER = [LAST] + list(range(8))
EPS = 1e-6
QR, CR, RD = 256, 128, 32
NOPE, VD, MH = 64, 64, 8
QD = NOPE + RD
SCALE = float(QD) ** -0.5
ZA = QR + CR + RD
HH, HK = 4, 128
HW = HH * HK
QSCALE = float(HK) ** -0.5
NG, EG, NE, FF = 4, 4, 16, 256
PAST = 256
KB = NT + PAST // P
SLOT_TILES = (2 * T) // P + NE
SLOTS = SLOT_TILES * P
NEG = -1e30
LEVELS = [1, 2, 4, 8, 16, 32, 64]

C_ID = 0
C_IDQ = C_ID + P
C_BD = C_IDQ + P
C_TRI = C_BD + HW
C_ONE = C_TRI + P
C_COS = C_ONE + P
C_SIN = C_COS + NT * 16
C_W4 = C_SIN + NT * 16
C_THR = C_W4 + 4
C_IOTA = C_THR + 9
C_VALID = C_IOTA + SLOT_TILES
C_TOK = C_VALID + NT
C_HALF = C_TOK + NT
C_END = C_HALF + NT * 4


def constants():
    import numpy as np
    c = np.zeros((P, C_END), np.float32)
    c[:, C_ID:C_ID + P] = np.eye(P)
    c[:, C_IDQ:C_IDQ + P] = np.eye(P) * QSCALE
    c[:, C_BD:C_BD + HW] = (np.arange(P)[:, None] // META == np.arange(HW)[None] // VD)
    c[:, C_TRI:C_TRI + P] = np.triu(np.ones((P, P)), 1)
    c[:, C_ONE:C_ONE + P] = 1.0
    pos = np.zeros((NT, P), np.float32)
    for t in range(8):
        pos[t] = META + t * P + np.arange(P)
    pos[LAST, :SAMPLE] = PAST + np.arange(SAMPLE)
    pos[LAST, SAMPLE:SAMPLE + META] = np.arange(META)
    inv = (np.float32(10000.0) ** (-np.arange(16, dtype=np.float32) / np.float32(16))).astype(np.float32)
    ang = (pos[:, :, None] * inv).astype(np.float32).transpose(1, 0, 2).reshape(P, NT * 16)
    c[:, C_COS:C_COS + NT * 16] = np.cos(ang.astype(np.float64))
    c[:, C_SIN:C_SIN + NT * 16] = np.sin(ang.astype(np.float64))
    c[:, C_W4:C_W4 + 4] = [4, 3, 2, 1]
    c[:, C_THR:C_THR + 9] = np.arange(9) * P
    c[:, C_IOTA:C_IOTA + SLOT_TILES] = np.arange(SLOT_TILES)
    for t in range(NT):
        c[:ROWS[t], C_VALID + t] = 1.0
        c[:, C_TOK + t] = t * P + np.arange(P)
    c[:, C_HALF:C_END] = -0.5
    m = np.zeros((P, len(LEVELS), 64), np.int32)
    s = np.arange(P)[:, None]
    for n, h in enumerate(LEVELS):
        k = np.arange(64)[None]
        t = (k // h) * 2 * h + h + k % h
        m[:, n] = (s // (2 * h) == t // (2 * h)) & (s % (2 * h) < h)
    return c, m.reshape(P, -1)


def hybrid_layer(nc, x_prompt, x_sample, cache_ckv, cache_krope, state_hgrn, meta_tokens, attn_norm, w_in, q_norm,
                 kv_norm, w_uq, w_uk, w_uv, hg_lb_logits, hg_gnorm, w_o, ffn_norm, w_router_group, b_router_group,
                 w_router_expert, b_router_expert, w1, w3, w2, final_norm, table, level_masks,
                 y_prompt, y_sample, ckv_prompt, krope_prompt, hgrn_prompt, ckv_sample, krope_sample, hgrn_sample):
    ctx = ExitStack()
    arena_floats = 53000
    parts_floats = 2 * KC * 2 * FF + 2 * 2 * D + KC * P + 2 * P
    with nc.sbuf_tensor("arena", [P, arena_floats], F32) as arena:
        pass
    below_floats = arena_floats - 2 * parts_floats
    below = ctx.enter_context(nc.sbuf_tensor("below", [P, below_floats], F32))
    high = ctx.enter_context(nc.sbuf_tensor("high", [P, parts_floats], F32R))
    low = ctx.enter_context(nc.sbuf_tensor("low", [P, parts_floats], F32R))
    ps = ctx.enter_context(nc.psum_tensor("ps", [P, 8, 512], F32))

    class Region:
        def __init__(self, base, of=arena, floats=arena_floats):
            self.at, self.of, self.floats = base, of, floats

        def take(self, *dims):
            n = 1
            for d in dims:
                n *= d
            a = self.of[:, self.at:self.at + n]
            self.at += n
            assert self.at <= self.floats, self.at
            if len(dims) == 2:
                a = a.rearrange("p (a b) -> p a b", a=dims[0])
            if len(dims) == 3:
                a = a.rearrange("p (a b c) -> p a b c", a=dims[0], b=dims[1])
            return a

    def sem(name):
        return ctx.enter_context(nc.semaphore(name))

    keep = Region(0)
    tab = keep.take(C_END)
    masks = keep.take(len(LEVELS) * 64).bitcast(I32)
    logits = keep.take(NT, NG + NE)
    stat = keep.take(64)
    hg_base = keep.at
    hg_out = keep.take(NT, HW)
    z_mla = keep.take(NT, ZA)
    ident = tab[:, C_ID:C_ID + P]
    ident_q = tab[:, C_IDQ:C_IDQ + P]
    ones = tab[:, C_ONE:C_ONE + P]
    neg_half = tab[:, C_HALF:C_HALF + NT * 4]

    r = Region(keep.at)
    v_hg = r.take(NT, HW)
    q_hg = r.take(HH, TP)
    f_hg = r.take(HH, TP)
    norm_base = r.at
    k_hg = r.take(HH, TP)
    gn_b = r.take(HK)
    lbl = r.take(2, HH)
    lb = r.take(4, HH)
    work_base = r.at
    x_t = r.take(KC, T)
    w_grp = r.take(2, KC, 512)
    r = Region(norm_base)
    x_row = r.take(2, D)
    xs = r.take(1, D)
    an_b = r.take(D)
    r = Region(work_base)
    q_lv = r.take(3, HH, P)
    k_lv = r.take(3, HH, P)
    tot = r.take(8, HH, 64)
    attn_t = r.take(2, HH, P)
    state = r.take(HH, HK)
    state_s = r.take(HH, HK)
    k_rows = r.take(HH, P)
    o_stat = r.take(2, HH)
    o_rstd = r.take(2, HH)

    r = Region(keep.at)
    k_t = r.take(MH, T + PAST)
    v_rows = r.take(KB, MH * VD)
    v_meta = r.take(MH * VD)
    ckv_t = r.take(T + PAST)
    cq_t = r.take(2, TP)
    wuq = r.take(2, MH * QD)
    wuk = r.take(MH * NOPE)
    wuv = r.take(MH * VD)
    wo = r.take(KC, D)
    wr = r.take(KC, NG + NE)
    br_b = r.take(NG + NE)
    fn_b = r.take(D)
    q_t = r.take(MH, P)
    q_row = r.take(MH, QD)
    rope_tmp = r.take(4, NT * 16)
    p_base = r.at
    p_rows = r.take(3, D)
    p_t = r.take(2, 4, P)
    pm_row = r.take(MH, META)
    nbias = r.take(2, MH)
    sm_stat = r.take(6, MH)
    h_base = r.at
    h_row = r.take(2, D)
    h_stat = r.take(2, 2)
    hn_row = r.take(D)
    r = Region(keep.at - NT * ZA)
    hn_t = r.take(KC, P)
    mix_t = r.take(KC, P)
    mix_row = r.take(HW)
    r = Region(p_base)
    kr96 = r.take(KB, 96)
    cache_c = r.take(2, CR)
    m8 = r.take(P)
    z_sq = r.take(NT, 2)
    r = Region(h_base)
    qn_b = r.take(QR)
    kvn_b = r.take(CR)
    z_junk = r.take(QR)

    r = Region(hg_base)
    rt = r.take(24, NT * NE)
    expert_of = r.take(SLOT_TILES).bitcast(I32)
    gates = r.take(2, NT)
    slot_i = r.take(2, NT).bitcast(I32)
    tok_rows = r.take(P)
    tok_i = r.take(SLOT_TILES).bitcast(I32)
    r = Region(r.at, below, below_floats)
    w13_in = r.take(KC, 2 * FF)
    w2_in = r.take(2, D)
    r = Region(r.at)
    xg = r.take(2, D)
    act_h = r.take(FF)
    g_row = r.take(FF)
    y_row = r.take(2, D)
    assert r.at <= below_floats
    hi, lo = Region(0, high, parts_floats), Region(0, low, parts_floats)
    (w13_hi, w13_lo), (w2_hi, w2_lo) = ([[q.take(*dims) for _ in range(2)] for q in (hi, lo)]
                                        for dims in ((KC, 2 * FF), (2, D)))
    (xg_hi, xg_lo), (g_hi, g_lo) = ([q.take(*dims) for q in (hi, lo)] for dims in ((KC, P), (2, P)))
    r = Region(keep.at + 8000)
    FB = 4
    res = r.take(FB, D)
    ya = r.take(FB, D)
    yb = r.take(FB, D)
    y_out = r.take(FB, D)
    fin_b = r.take(D)
    y_sq = r.take(D)
    y_stat = r.take(2, NT)

    h1_dram = nc.dram_tensor("h1_dram", [T, D], F32).ap()
    hn_dram = nc.dram_tensor("hn_dram", [T, D], F32).ap()
    tok_dram = nc.dram_tensor("tok_dram", [SLOTS, 1], F32).ap()
    y_dram = nc.dram_tensor("y_dram", [SLOTS, D], F32).ap()

    phase_end = sem("phase_end")
    phases = {"n": 0}

    def end_phase(eng, n):
        eng.drain().then_inc(phase_end, 1)
        eng.wait_ge(phase_end, 4 * (n + 1))

    s_tab = sem("s_tab")
    s_xrow = [sem(f"s_xrow{i}") for i in range(2)]
    s_norm_w = sem("s_norm_w")
    s_ssq = sem("s_ssq")
    s_rstd = sem("s_rstd")
    s_xs = sem("s_xs")
    s_xps = sem("s_xps")
    s_xta = sem("s_xta")
    s_xtv = sem("s_xtv")
    s_wg = [sem(f"s_wg{i}") for i in range(2)]
    s_zps = sem("s_zps")
    s_zev = sem("s_zev")
    s_zero = sem("s_zero")
    s_lb = sem("s_lb")
    s_lbe = sem("s_lbe")
    s_fk = sem("s_fk")
    s_gs = sem("s_gs")

    c0 = ZA
    GROUPS = [("mla", 0, ZA), ("v", c0 + 2 * HW, HW), ("gate", c0 + 3 * HW, HW), ("f", c0 + HW, HW), ("q", c0, HW)]
    Z_OUT = []
    for g, (kind, _, _) in enumerate(GROUPS):
        if kind in ("f", "q"):
            Z_OUT += [(kind, g, m, n) for m in range(HH) for n in range(3)]
        else:
            Z_OUT += [(kind, g, t, 0) for t in range(NT)]
    ZN = T // 3
    Z_RING = 6

    s_hin = sem("s_hin")
    s_init = sem("s_init")
    s_lvl = sem("s_lvl")
    s_cpy = sem("s_cpy")
    s_prod = sem("s_prod")
    s_mask = sem("s_mask")
    s_ops = sem("s_ops")
    s_osq = sem("s_osq")
    s_ors = sem("s_ors")
    s_oev = sem("s_oev")
    s_ktp = sem("s_ktp")
    s_kte = sem("s_kte")
    s_sps = sem("s_sps")
    s_sev = sem("s_sev")
    s_st0 = sem("s_st0")

    s_out = sem("s_out")
    outs = {"n": 0}


    def col0(t):
        return t * P

    def levels(c):
        return LEVELS[:6] if c == LAST else LEVELS

    LV0 = [sum(len(levels(c)) for c in ORDER[:i]) for i in range(NT + 1)]
    PR0 = [sum(len(levels(c)) + 1 for c in ORDER[:i]) for i in range(NT + 1)]

    def x_half(act, t):
        act.wait_ge(s_xps, 2 * t + 1)
        act.activation(x_t[:, 0:4, col0(t):col0(t) + ROWS[t]],
                       ps[:, 6, :].rearrange("p (a b) -> p a b", a=4)[:, :, 0:ROWS[t]], ACT.Copy).then_inc(s_xta, 1)

    s_pool = sem("s_pool")
    pool_chain = [0]
    s_dve = sem("s_dve")
    dve_chain = [0]

    def key_col(kb):
        return kb * P if kb < NT else T + (kb - NT) * P

    def key_rows(kb):
        return ROWS[kb] if kb < NT else P

    MCOL = LAST * P + SAMPLE

    def main_blocks(t):
        return [(NT, P), (NT + 1, P), (LAST, SAMPLE)] if t == LAST else [(kb, P) for kb in range(t + 1)]

    def main_width(t):
        return sum(w for _, w in main_blocks(t))

    STEPS = [("kb", kb, 0) for kb in range(KB)]
    KN = [(0, 512), (512, 512), (1024, T + PAST - 1024)]
    STEPS += [("kn", hd, n) for hd in range(MH) for n in range(3)]
    STEPS += [("v", kb, 0) for kb in range(KB)] + [("vm", 0, 0), ("q", 0, 0), ("qt", 0, 0)]
    for i in range(NT):
        STEPS.append(("meta", i, 0))
        for hd in range(MH):
            STEPS.append(("score", i, hd))
            side = {1: "wot", 2: "wo", 3: "sq", 4: "hn", 5: "hnt", 6: "rt"}.get(hd)
            if i and side:
                STEPS.append((side, i - 1, 0))
            if hd == 3 and i + 1 < NT:
                STEPS.append(("q", i + 1, 0))
            if hd >= 2:
                STEPS.append(("attn", i, hd - 2))
        STEPS += [("attn", i, 6), ("attn", i, 7), ("mpv", i, 0)]
        if i + 1 < NT:
            STEPS.append(("qt", i + 1, 0))
    STEPS += [(s, NT - 1, 0) for s in ("wot", "wo", "sq", "hn", "hnt", "rt")]

    STEPS_ACT = []
    held = None
    for st in STEPS:
        if st[0] == "score" and st[2] >= 2:
            held = st
            continue
        STEPS_ACT.append(st)
        if st[0] == "attn" and held:
            STEPS_ACT.append(held)
            held = None

    S_JOB = {}
    PT_GROUP = {}
    P_INDEX = {}
    for st in STEPS:
        kind, i, hd = st
        if kind in ("kn", "v", "vm", "q", "score", "wo", "rt"):
            S_JOB[st] = len(S_JOB)
        if kind == "kb":
            PT_GROUP[st + (0,)] = len(PT_GROUP)
        if kind in ("qt", "wot", "hnt"):
            for half in range(2):
                PT_GROUP[st + (half,)] = len(PT_GROUP)
        if kind == "attn":
            for g in range((len(main_blocks(ORDER[i])) + 3) // 4):
                PT_GROUP[st + (g,)] = len(PT_GROUP)
                P_INDEX[st + (g,)] = len(P_INDEX)
        if kind == "mpv":
            PT_GROUP[st + (0,)] = len(PT_GROUP)
            P_INDEX[st + (0,)] = len(P_INDEX)

    def last_group(a):
        i, hd = divmod(a, MH)
        return PT_GROUP[("attn", i, hd, (len(main_blocks(ORDER[i])) + 3) // 4 - 1)]

    s_wat = sem("s_wat")
    s_nw = sem("s_nw")
    s_cch = sem("s_cch")
    s_zsq = sem("s_zsq")
    s_zrs = sem("s_zrs")
    s_kr0 = sem("s_kr0")
    s_zn = sem("s_zn")
    s_sps2 = sem("s_sjob")
    s_srel = [sem(f"s_srel{i}") for i in range(2)]
    s_pt = sem("s_pt")
    s_ptrel = [sem(f"s_ptrel{i}") for i in range(2)]
    s_m8 = sem("s_m8")
    s_kv_out = sem("s_kv_out")
    s_qrope = sem("s_qrope")
    s_meta = sem("s_meta")
    s_nb = sem("s_nb")
    s_pused = sem("s_pused")
    s_dm = sem("s_dm")
    s_pm = sem("s_pm")
    s_o = sem("s_o")
    s_mix = sem("s_mix")
    s_xres = [sem(f"s_xres{i}") for i in range(2)]
    s_h1st = sem("s_h1st")
    s_hsq = sem("s_hsq")
    s_hrs = sem("s_hrs")
    s_hn = sem("s_hn")
    s_hnst = sem("s_hnst")

    def s_banks(st):
        return 2 * (S_JOB[st] % 2)

    def s_wait_free(pe, st):
        k = S_JOB[st]
        if k >= 2:
            pe.wait_ge(s_srel[k % 2], k // 2)

    def s_wait_read(eng, st):
        k = S_JOB[st]
        eng.wait_ge(s_srel[k % 2], k // 2 + 1)

    def pt_wait_free(pe, key):
        k = PT_GROUP[key]
        if k >= 2:
            pe.wait_ge(s_ptrel[k % 2], k // 2)

    def pt_wait_done(eng, key):
        k = PT_GROUP[key]
        eng.wait_ge(s_ptrel[k % 2], k // 2 + 1)

    def copies_it(key, who):
        return (PT_GROUP[key] % 2 == 0) == (who == "act")

    def evacuate(eng, who, st):
        kind, i, hd = st
        t = ORDER[i] if i < NT else 0
        R = ROWS[t]
        cp = (lambda o, a: eng.activation(o, a, ACT.Copy)) if who == "act" else eng.tensor_copy
        keys = [k for k in (st + (g,) for g in range(2)) if k in PT_GROUP]
        for key in keys:
            if not copies_it(key, who):
                continue
            g = PT_GROUP[key]
            eng.wait_ge(s_pt, g + 1)
            src = ps[:, 4 + g % 2, :].rearrange("p (a b) -> p a b", a=4)
            rel = s_ptrel[g % 2]
            half = key[3]
            if kind == "kb":
                n, c = key_rows(i), key_col(i)
                if i < NT:
                    cp(cq_t[:, :, c:c + n], src[:, 0:2, 0:n])
                cp(ckv_t[:, c:c + n], src[:, 2, 0:n])
                cp(k_t[64:96, :, c:c + n], src[64:96, 3, 0:n].unsqueeze(1).to_broadcast([32, MH, n])).then_inc(rel, 1)
            elif kind == "qt":
                cp(q_t[0:QD, 4 * half:4 * half + 4, 0:R], src[0:QD, :, 0:R]).then_inc(rel, 1)
            elif kind in ("wot", "hnt"):
                if kind == "wot":
                    eng.wait_ge(s_kv_out, 16 * 6)
                dst = mix_t if kind == "wot" else hn_t
                cp(dst[:, 4 * half:4 * half + 4, 0:R], src[:, :, 0:R]).then_inc(rel, 1)
            else:
                ip = P_INDEX[key]
                if ip >= 2:
                    eng.wait_ge(s_pused, ip - 1)
                if kind == "mpv":
                    cp(p_t[:, ip % 2, 0, 0:R], src[:, 0, 0:R]).then_inc(rel, 1)
                else:
                    bl = main_blocks(t)[4 * half:4 * half + 4]
                    full = [b for b in bl if b[1] == P]
                    ins = cp(p_t[:, ip % 2, 0:len(full), 0:R], src[:, 0:len(full), 0:R])
                    if len(full) < len(bl):
                        ins = cp(p_t[0:SAMPLE, ip % 2, len(full), 0:R], src[0:SAMPLE, len(full), 0:R])
                    ins.then_inc(rel, 1)

    def attention_loads(sp):
        sp.wait_ge(phase_end, 8)
        sp.dma_start(cache_c, cache_ckv[0, 0].rearrange("(b p) c -> p b c", p=P)).then_inc(s_cch, 16)
        sp.dma_start(kr96[:, NT:KB, 64:96], cache_krope[0, 0].rearrange("(b p) c -> p b c", p=P)).then_inc(s_cch, 16)
        sp.dma_start(qn_b, q_norm[0:1, :].to_broadcast([P, QR])).then_inc(s_nw, 16)
        sp.dma_start(kvn_b, kv_norm[0:1, :].to_broadcast([P, CR])).then_inc(s_nw, 16)
        sp.dma_start(wuk, w_uk[0].rearrange("c h n -> c (h n)")).then_inc(s_wat, 16)
        sp.dma_start(wuv, w_uv[0].rearrange("c h n -> c (h n)")).then_inc(s_wat, 16)
        sp.dma_start(wuq, w_uq[0].rearrange("(c p) h n -> p c (h n)", p=P)).then_inc(s_wat, 16)
        sp.dma_start(wo, w_o[0].rearrange("(c p) n -> p c n", p=P)).then_inc(s_wat, 16)
        sp.dma_start(wr[:, :, 0:NG], w_router_group[0].rearrange("(c p) n -> p c n", p=P),
                     allow_slow_non_contiguous=True).then_inc(s_wat, 16)
        sp.dma_start(wr[:, :, NG:], w_router_expert[0].rearrange("(c p) n -> p c n", p=P),
                     allow_slow_non_contiguous=True).then_inc(s_wat, 16)
        sp.dma_start(br_b[:, 0:NG], b_router_group[0:1, :].to_broadcast([P, NG])).then_inc(s_wat, 16)
        sp.dma_start(br_b[:, NG:], b_router_expert[0:1, :].to_broadcast([P, NE])).then_inc(s_wat, 16)
        sp.dma_start(fn_b, ffn_norm[0:1, :].to_broadcast([P, D])).then_inc(s_wat, 16)
        sp.wait_ge(s_zn, 3)
        lat = z_mla[:, :, QR:QR + CR]
        rop = kr96[:, :, 64:96]
        for dst_p, dst_s, src in ((ckv_prompt, ckv_sample, lat), (krope_prompt, krope_sample, rop)):
            sp.dma_start(dst_p[0, 0, META:, :].rearrange("(t p) c -> p t c", p=P), src[:, 0:8, :]).then_inc(s_kv_out, 16)
            sp.dma_start(dst_p[0, 0, 0:META, :], src[SAMPLE:SAMPLE + META, LAST, :]).then_inc(s_kv_out, 16)
            sp.dma_start(dst_s[0, 0], src[0:SAMPLE, LAST, :]).then_inc(s_kv_out, 16)
        sp.wait_ge(s_kv_out, 16 * 6)

        def load_residual(i):
            t = ORDER[i]
            if t < 8:
                sp.dma_start(h_row[:, i % 2, :], x_prompt[0, t * P:(t + 1) * P, :]).then_inc(s_xres[i % 2], 32)
            else:
                sp.dma_start(h_row[0:SAMPLE, i % 2, :], x_sample[0]).then_inc(s_xres[i % 2], 16)
                sp.dma_start(h_row[SAMPLE:SAMPLE + META, i % 2, :], meta_tokens).then_inc(s_xres[i % 2], 16)

        load_residual(0)
        load_residual(1)
        for i in range(NT):
            t, R = ORDER[i], ROWS[ORDER[i]]
            s_wait_read(sp, ("wo", i, 0))
            sp.dma_start(h1_dram[t * P:t * P + R, :], h_row[0:R, i % 2, :]).then_inc(s_h1st, 16)
            sp.wait_ge(s_hn, i + 1)
            sp.dma_start(hn_dram[t * P:t * P + R, :], hn_row[0:R, :]).then_inc(s_hnst, 16)
            if i + 2 < NT:
                sp.wait_ge(s_h1st, 16 * (i + 1))
                load_residual(i + 2)

    def attention_pool(pool, rsqrt_mean):
        pool.memset(kr96[:, :, 0:64], 0.0).then_inc(s_kr0, 1)
        rsqrt_mean(z_sq.rearrange("p a b -> p (a b)")[:, 0:NT], z_sq.rearrange("p a b -> p (a b)")[:, 0:NT], QR, s_zsq,
                   s_zrs, 2 * NT)
        rsqrt_mean(z_sq.rearrange("p a b -> p (a b)")[:, NT:2 * NT], z_sq.rearrange("p a b -> p (a b)")[:, NT:2 * NT],
                   CR, s_zsq, s_zrs, 2 * NT)
        for i in range(NT):
            R = ROWS[ORDER[i]]
            rsqrt_mean(h_stat[0:R, i % 2, 1:2], h_stat[0:R, i % 2, 0:1], D, s_hsq, s_hrs, i + 1)

    def attention_act(act):
        for t in range(NT):
            if t:
                act.wait_ge(s_zsq, 2 * t)
            act.activation(z_junk[:, 0:QR], z_mla[:, t, 0:QR], ACT.Square,
                           accum_out=z_sq.rearrange("p a b -> p (a b)")[:, t:t + 1]).then_inc(s_zsq, 1)
            act.wait_ge(s_zsq, 2 * t + 1)
            act.activation(z_junk[:, 0:CR], z_mla[:, t, QR:QR + CR], ACT.Square,
                           accum_out=z_sq.rearrange("p a b -> p (a b)")[:, NT + t:NT + t + 1]).then_inc(s_zsq, 1)
        for st in STEPS_ACT:
            kind, i, hd = st
            t = ORDER[i] if i < NT else 0
            R = ROWS[t]
            if kind != "mpv":
                evacuate(act, "act", st)
            if st in S_JOB:
                k = S_JOB[st]
                bank = s_banks(st)
                if kind in ("kn", "v") and k % 2 == 0:
                    act.wait_ge(s_sps2, k + 1)
                    if kind == "kn":
                        c, n = KN[hd]
                        act.activation(k_t[0:64, i, c:c + n], ps[0:64, bank, 0:n], ACT.Copy).then_inc(s_srel[0], 1)
                    else:
                        n = key_rows(i)
                        act.activation(v_rows[0:n, i, :], ps[0:n, bank, :], ACT.Copy).then_inc(s_srel[0], 1)
                if kind == "q":
                    act.wait_ge(s_sps2, k + 1)
                    act.activation(q_row[0:R].rearrange("p (c h) d -> p c (h d)", c=2), ps[0:R, bank:bank + 2, 0:4 * QD],
                                   ACT.Copy).then_inc(s_srel[k % 2], 1)
                if kind == "score":
                    a = i * MH + hd
                    w = main_width(t)
                    act.wait_ge(s_nb, a + 1)
                    if a == 0:
                        act.wait_ge(s_kv_out, 16 * 6)
                    if a >= 3:
                        act.wait_ge(s_pt, last_group(a - 3) + 1)
                    act.activation(p_rows[0:R, a % 3, 0:w],
                                   ps[0:R, bank:bank + 2, :].rearrange("p a b -> p (a b)")[:, 0:w], ACT.Exp,
                                   bias=nbias[0:R, i % 2, hd:hd + 1], scale=SCALE,
                                   accum_out=sm_stat[0:R, 2, hd:hd + 1]).then_inc(s_srel[k % 2], 1)
            if kind == "mpv":
                act.wait_ge(s_dm, i + 1)
                act.activation(pm_row[0:R], pm_row[0:R], ACT.Exp).then_inc(s_pm, 1)
                evacuate(act, "act", st)
            if kind == "sq":
                s_wait_read(act, ("wo", i, 0))
                if i:
                    act.wait_ge(s_hnst, 16 * i)
                    act.wait_ge(s_pt, PT_GROUP[("hnt", i - 1, 0, 1)] + 1)
                act.activation(hn_row[0:R], h_row[0:R, i % 2, :], ACT.Square,
                               accum_out=h_stat[0:R, i % 2, 0:1]).then_inc(s_hsq, 1)

    def attention_pe(pe):
        pending = []

        def turn(key, blocks, waits=()):
            pt_wait_free(pe, key)
            g = PT_GROUP[key]
            for n, (src, rows, width) in enumerate(blocks):
                if src is not None:
                    ins = pe.transpose(ps[0:width, 4 + g % 2, n * P:n * P + rows], src, ident[0:rows, 0:rows])
            return ins.then_inc(s_pt, 1)

        def weigh():
            key = pending.pop(0)
            kind, i, hd, g = key
            t = ORDER[i]
            R = ROWS[t]
            pt_wait_done(pe, key)
            ip = P_INDEX[key]
            if kind == "mpv":
                pe.matmul(ps[0:R, 6, :], p_t[:, ip % 2, 0, 0:R], v_meta, start=False, stop=True,
                          skip_group_check=True).then_inc(s_pused, 1)
                return
            if i and hd == 0 and g == 0:
                pe.wait_ge(s_mix, i)
            for n, (kb, w) in enumerate(main_blocks(t)[4 * g:4 * g + 4]):
                ins = pe.matmul(ps[0:R, 6, hd * VD:(hd + 1) * VD], p_t[0:w, ip % 2, n, 0:R],
                                v_rows[0:w, kb, hd * VD:(hd + 1) * VD],
                                start=hd == 0 and g == 0 and n == 0, stop=False, skip_group_check=True)
            ins.then_inc(s_pused, 1)

        pe.wait_ge(s_zn, 3)
        pe.wait_ge(s_cch, 32)
        for st in STEPS:
            kind, i, hd = st
            t = ORDER[i] if i < NT else 0
            R = ROWS[t]
            if st in S_JOB:
                s_wait_free(pe, st)
                bank = s_banks(st)
            if kind == "kb":
                n = key_rows(i)
                rows = slice(0, n)
                if i < NT:
                    bl = [(z_mla[rows, i, 0:P], n, P), (z_mla[rows, i, P:2 * P], n, P),
                          (z_mla[rows, i, QR:QR + CR], n, P)]
                else:
                    bl = [(None, 0, 0), (None, 0, 0), (cache_c[:, i - NT, :], n, P)]
                turn(st + (0,), bl + [(kr96[rows, i, :], n, 96)])
            if kind == "kn":
                if i == 0 and hd == 0:
                    pe.wait_ge(s_wat, 16 * 9)
                    for kb in range(KB):
                        pt_wait_done(pe, ("kb", kb, 0, 0))
                c, n = KN[hd]
                pe.matmul(ps[0:NOPE, bank, 0:n], wuk[:, i * NOPE:(i + 1) * NOPE], ckv_t[:, c:c + n],
                          start=True, stop=True).then_inc(s_sps2, 1)
            if kind == "v":
                c, n = key_col(i), key_rows(i)
                pe.matmul(ps[0:n, bank, :], ckv_t[:, c:c + n], wuv, start=True, stop=True).then_inc(s_sps2, 1)
            if kind == "vm":
                pe.wait_ge(s_m8, 1)
                pe.matmul(ps[:, bank, :], m8, wuv, start=True, stop=True).then_inc(s_sps2, 1)
            if kind == "q":
                for n in range(2):
                    for kk in range(2):
                        ins = pe.matmul(ps[0:R, bank + n, 0:4 * QD], cq_t[:, kk, col0(t):col0(t) + R],
                                        wuq[:, kk, n * 4 * QD:(n + 1) * 4 * QD], start=kk == 0, stop=kk == 1)
                ins.then_inc(s_sps2, 1)
            if kind == "qt":
                pe.wait_ge(s_qrope, i + 1)
                for half in range(2):
                    turn(st + (half,), [(q_row[0:R, 4 * half + n, :], R, QD) for n in range(4)])
            if kind == "meta":
                pt_wait_done(pe, ("qt", i, 0, 0))
                pt_wait_done(pe, ("qt", i, 0, 1))
                if i:
                    pe.wait_ge(s_dm, i)
                else:
                    for k in range(2):
                        last = max(v for s_, v in S_JOB.items() if s_[0] in ("kn", "v", "vm") and v % 2 == k)
                        pe.wait_ge(s_srel[k], last // 2 + 1)
                for h_ in range(MH):
                    ins = pe.matmul(ps[0:R, 7, h_ * META:(h_ + 1) * META], q_t[0:QD, h_, 0:R],
                                    k_t[0:QD, h_, MCOL:MCOL + META], start=True, stop=True)
                ins.then_inc(s_meta, 1)
            if kind == "score":
                if t == LAST:
                    pe.matmul(ps[0:R, bank, 0:PAST], q_t[0:QD, hd, 0:R], k_t[0:QD, hd, T:T + PAST],
                              start=True, stop=True)
                    ins = pe.matmul(ps[0:R, bank, PAST:PAST + SAMPLE], q_t[0:QD, hd, 0:R],
                                    k_t[0:QD, hd, LAST * P:LAST * P + SAMPLE], start=True, stop=True)
                else:
                    w = main_width(t)
                    for n in range(0, w, 512):
                        m = min(512, w - n)
                        ins = pe.matmul(ps[0:R, bank + n // 512, 0:m], q_t[0:QD, hd, 0:R],
                                        k_t[0:QD, hd, n:n + m], start=True, stop=True)
                ins.then_inc(s_sps2, 1)
            if kind == "attn":
                a = i * MH + hd
                bl = main_blocks(t)
                s_wait_read(pe, ("score", i, hd))
                for g in range((len(bl) + 3) // 4):
                    key = st + (g,)
                    ins = turn(key, [(p_rows[0:R, a % 3, (4 * g + n) * P:(4 * g + n) * P + w], R, w)
                                     for n, (_, w) in enumerate(bl[4 * g:4 * g + 4])])
                    if pending:
                        weigh()
                    pending.append(key)
            if kind == "mpv":
                while pending:
                    weigh()
                pe.wait_ge(s_pm, i + 1)
                turn(st + (0,), [(pm_row[0:R].rearrange("p h m -> p (h m)"), R, P)])
                pending.append(st + (0,))
                weigh()
            if kind == "wot":
                pe.wait_ge(s_mix, i + 1)
                for half in range(2):
                    src = mix_row if half == 0 else hg_out[:, t, :]
                    turn(st + (half,), [(src[0:R, n * P:(n + 1) * P], R, P) for n in range(4)])
            if kind == "wo":
                pt_wait_done(pe, ("wot", i, 0, 0))
                pt_wait_done(pe, ("wot", i, 0, 1))
                for n in range(2):
                    for kc in range(KC):
                        ins = pe.matmul(ps[0:R, bank + n, :], mix_t[:, kc, 0:R], wo[:, kc, n * 512:(n + 1) * 512],
                                        start=kc == 0, stop=kc == KC - 1)
                ins.then_inc(s_sps2, 1)
            if kind == "hnt":
                pe.wait_ge(s_hn, i + 1)
                for half in range(2):
                    turn(st + (half,), [(hn_row[0:R, (4 * half + n) * P:(4 * half + n + 1) * P], R, P)
                                        for n in range(4)])
            if kind == "rt":
                pt_wait_done(pe, ("hnt", i, 0, 0))
                pt_wait_done(pe, ("hnt", i, 0, 1))
                for kc in range(KC):
                    ins = pe.matmul(ps[0:R, bank, 0:NG + NE], hn_t[:, kc, 0:R], wr[:, kc, :],
                                    start=kc == 0, stop=kc == KC - 1)
                ins.then_inc(s_sps2, 1)

    def attention_dve(dve, link):
        dve.wait_ge(s_nw, 32)
        dve.wait_ge(s_zrs, 2)
        dve.wait_ge(s_kr0, 1)
        zq = z_sq.rearrange("p a b -> p (a b)")
        cq, ck = z_mla[:, :, 0:QR], z_mla[:, :, QR:QR + CR]
        link(dve.tensor_tensor(cq, cq, zq[:, 0:NT].unsqueeze(2).to_broadcast([P, NT, QR]), ALU.mult))
        dve.tensor_tensor(cq, cq, qn_b.unsqueeze(1).to_broadcast([P, NT, QR]), ALU.mult).then_inc(s_zn, 1)
        link(dve.tensor_tensor(ck, ck, zq[:, NT:2 * NT].unsqueeze(2).to_broadcast([P, NT, CR]), ALU.mult))
        dve.tensor_tensor(ck, ck, kvn_b.unsqueeze(1).to_broadcast([P, NT, CR]), ALU.mult).then_inc(s_zn, 1)
        c3 = tab[:, C_COS:C_COS + NT * 16].rearrange("p (t r) -> p t r", t=NT)
        s3 = tab[:, C_SIN:C_SIN + NT * 16].rearrange("p (t r) -> p t r", t=NT)

        def rope(x1, x2, cos, sin, o1, o2, n, R, done):
            tm = [rope_tmp[0:R, k, 0:n * 16].rearrange("p (a b) -> p a b", a=n) for k in range(4)]
            dve.tensor_tensor(tm[0], x1, cos, ALU.mult)
            dve.tensor_tensor(tm[1], x2, sin, ALU.mult)
            dve.tensor_tensor(tm[2], x2, cos, ALU.mult)
            link(dve.tensor_tensor(tm[3], x1, sin, ALU.mult))
            dve.tensor_tensor(o1, tm[0], tm[1], ALU.subtract)
            dve.tensor_tensor(o2, tm[2], tm[3], ALU.add).then_inc(done, 1)

        rope(z_mla[:, :, QR + CR:QR + CR + 16], z_mla[:, :, QR + CR + 16:ZA], c3, s3, kr96[:, 0:NT, 64:80],
             kr96[:, 0:NT, 80:96], NT, P, s_zn)
        for st in STEPS:
            kind, i, hd = st
            t = ORDER[i] if i < NT else 0
            R = ROWS[t]
            if kind != "mpv":
                evacuate(dve, "dve", st)
            if st in S_JOB:
                k = S_JOB[st]
                bank = s_banks(st)
                rel = s_srel[k % 2]
                if kind in ("kn", "v") and k % 2 == 1:
                    dve.wait_ge(s_sps2, k + 1)
                    if kind == "kn":
                        c, n = KN[hd]
                        dve.tensor_copy(k_t[0:64, i, c:c + n], ps[0:64, bank, 0:n]).then_inc(rel, 1)
                    else:
                        n = key_rows(i)
                        dve.tensor_copy(v_rows[0:n, i, :], ps[0:n, bank, :]).then_inc(rel, 1)
                if kind == "vm":
                    dve.wait_ge(s_sps2, k + 1)
                    dve.tensor_tensor(v_meta, ps[:, bank, :], tab[:, C_BD:C_BD + HW], ALU.mult).then_inc(rel, 1)
                if kind == "kn" and i == 0 and hd == 0:
                    pt_wait_done(dve, ("kb", LAST, 0, 0))
                    dve.tensor_copy(m8.rearrange("p (h m) -> p h m", h=MH),
                                    ckv_t[:, MCOL:MCOL + META].unsqueeze(1).to_broadcast([P, MH, META])
                                    ).then_inc(s_m8, 1)
                if kind == "q":
                    s_wait_read(dve, st)
                    sm3 = [a[0:R, t, :].unsqueeze(1).to_broadcast([R, MH, 16]) for a in (c3, s3)]
                    q1, q2 = q_row[0:R, :, NOPE:NOPE + 16], q_row[0:R, :, NOPE + 16:QD]
                    rope(q1, q2, sm3[0], sm3[1], q1, q2, MH, R, s_qrope)
                if kind == "score":
                    a = i * MH + hd
                    w = main_width(t)
                    dve.wait_ge(s_sps2, k + 1)
                    if hd == 0:
                        dve.wait_ge(s_meta, i + 1)
                        if t == LAST:
                            link(dve.memset(ps[0:SAMPLE, 7, 0:MH * META], NEG))
                        dve.tensor_reduce(sm_stat[0:R, 1, :],
                                          ps[0:R, 7, 0:MH * META].rearrange("p (h m) -> p h m", h=MH), AX.X, ALU.max)
                    S = ps[:, bank:bank + 2, :].rearrange("p a b -> p (a b)")
                    if t == LAST:
                        link(dve.memset(S[SAMPLE:R, 0:w], NEG))
                    else:
                        link(dve.memset(S[0:64, w - 64:w], NEG))
                    link(dve.tensor_reduce(sm_stat[0:R, 0, hd:hd + 1], S[0:R, 0:w], AX.X, ALU.max))
                    dve.tensor_scalar(nbias[0:R, i % 2, hd:hd + 1], sm_stat[0:R, 0, hd:hd + 1],
                                      sm_stat[0:R, 1, hd:hd + 1], -SCALE, ALU.max, ALU.mult).then_inc(s_nb, 1)
                if kind == "wo":
                    dve.wait_ge(s_sps2, k + 1)
                    dve.wait_ge(s_xres[i % 2], 32 * (i // 2 + 1))
                    h3 = h_row[0:R, i % 2, :].rearrange("p (a b) -> p a b", a=2)
                    dve.tensor_tensor(h3, h3, ps[0:R, bank:bank + 2, :], ALU.add).then_inc(rel, 1)
                if kind == "rt":
                    dve.wait_ge(s_sps2, k + 1)
                    dve.tensor_tensor(logits[0:R, t, :], ps[0:R, bank, 0:NG + NE], br_b[0:R, :],
                                      ALU.add).then_inc(rel, 1)
            if kind == "mpv":
                mrow = ps[0:R, 7, 0:MH * META].rearrange("p (h m) -> p h m", h=MH)
                dve.wait_ge(s_nb, (i + 1) * MH)
                dve.scalar_tensor_tensor(out=pm_row[0:R], in0=mrow, scalar=SCALE,
                                         in1=nbias[0:R, i % 2, :].unsqueeze(2).to_broadcast([R, MH, META]),
                                         op0=ALU.mult, op1=ALU.add).then_inc(s_dm, 1)
                dve.wait_ge(s_pm, i + 1)
                s_wait_read(dve, ("score", i, MH - 1))
                link(dve.tensor_reduce(sm_stat[0:R, 3, :], pm_row[0:R], AX.X, ALU.add))
                link(dve.tensor_tensor(sm_stat[0:R, 3, :], sm_stat[0:R, 3, :], sm_stat[0:R, 2, :], ALU.add))
                link(dve.reciprocal(sm_stat[0:R, 4, :], sm_stat[0:R, 3, :]))
                evacuate(dve, "dve", st)
                dve.wait_ge(s_pused, P_INDEX[st + (0,)] + 1)
                dve.tensor_tensor(mix_row[0:R, :].rearrange("p (h v) -> p h v", h=MH),
                                  ps[0:R, 6, :].rearrange("p (h v) -> p h v", h=MH),
                                  sm_stat[0:R, 4, :].unsqueeze(2).to_broadcast([R, MH, VD]), ALU.mult
                                  ).then_inc(s_mix, 1)
            if kind == "hn":
                dve.wait_ge(s_hrs, i + 1)
                dve.scalar_tensor_tensor(out=hn_row[0:R], in0=h_row[0:R, i % 2, :], scalar=h_stat[0:R, i % 2, 1:2],
                                         in1=fn_b[0:R, :], op0=ALU.mult, op1=ALU.mult).then_inc(s_hn, 1)

    s_rexp_in = sem("s_rexp_in")
    s_rexp = sem("s_rexp")
    s_cnt = sem("s_cnt")
    s_rank = sem("s_rank")
    s_slots = sem("s_slots")
    s_etab = sem("s_etab")
    s_tok0 = sem("s_tok0")
    s_tokz = sem("s_tokz")
    s_scat = sem("s_scat")
    s_tokr = sem("s_tokr")
    s_tokt = sem("s_tokt")
    s_toki = sem("s_toki")
    s_w13in = [sem(f"s_w13in{i}") for i in range(4)]
    s_w2in = [sem(f"s_w2in{i}") for i in range(2)]
    s_w13hi = sem("s_w13hi")
    s_w13lo = sem("s_w13lo")
    s_w2hi = sem("s_w2hi")
    s_w2lo = sem("s_w2lo")
    s_xg = [sem(f"s_xg{i}") for i in range(2)]
    s_yst = [sem(f"s_yst{i}") for i in range(2)]
    s_mx = sem("s_mx")
    s_mxa = sem("s_mxa")
    s_mxv = sem("s_mxv")
    s_mh = sem("s_mh")
    s_ms = sem("s_ms")
    s_mg = sem("s_mg")
    s_mgt = sem("s_mgt")
    s_mga = sem("s_mga")
    s_mgv = sem("s_mgv")
    s_my = sem("s_my")
    s_mya = sem("s_mya")
    s_myv = sem("s_myv")
    s_fin_w = sem("s_fin_w")
    s_res = [sem(f"s_res{i}") for i in range(FB)]
    s_yab = [sem(f"s_yab{i}") for i in range(FB)]
    s_comb = sem("s_comb")
    s_ysq = sem("s_ysq")
    s_yrs = sem("s_yrs")
    s_yo = sem("s_yo")
    s_yout = [sem(f"s_yout{i}") for i in range(FB)]
    UN = 2
    WC = 4

    def uses(j):
        return len(range(j, SLOT_TILES, UN))

    def expert_turns(eng, body):
        turns = SLOT_TILES // UN
        for it in range(2):
            for j in range(UN):
                body(it, j, it == 0, False)
        with eng.Fori(2, turns) as it:
            for j in range(UN):
                body(it, j, False, False)
        assert SLOT_TILES % UN == 1
        body(turns, 0, False, True)

    def is_zero(s):
        return isinstance(s, int) and s == 0

    def chunk(w, c):
        return w[:, 2 * c:2 * c + 2, :]

    def expert(eng, s):
        e = eng.value_load(expert_of[0:1, bass.ds(s, 1)], min_val=0, max_val=NE - 1)
        if is_zero(s):
            return e, None
        return e, e != eng.value_load(expert_of[0:1, bass.ds(s - 1, 1)], min_val=0, max_val=NE - 1)

    def moe_loads(sp):
        sp.wait_ge(s_tok0, 1)
        sp.dma_start(tok_dram.rearrange("(p s) o -> p (s o)", p=P), tok_rows[:, 0:SLOT_TILES]).then_inc(s_tokz, 16)
        sp.wait_ge(s_scat, 16 * 2 * NT)
        sp.dma_start(tok_rows[0:SLOT_TILES, :], tok_dram.rearrange("(s p) o -> s (p o)", p=P)).then_inc(s_tokr, 16)
        sp.wait_ge(s_etab, 1)

        def body(it, j, first, last):
            s = it * UN + j
            e, new = expert(sp, s)
            rows13 = [w[0, bass.ds(e, 1)].rearrange("e (c p) f -> p (e c) f", p=P) for w in (w1, w3)]
            for c in range(WC):
                if not is_zero(s):
                    split = sp.to_reg(WC * (s - 1) + c + 1)
                    if c == 0:
                        sp.wait_ge(s_etab, 1)
                    sp.wait_ge(s_w13lo, split)
                for k in range(2):
                    sp.dma_start(w13_in[:, 2 * c:2 * c + 2, k * FF:(k + 1) * FF], rows13[k][:, 2 * c:2 * c + 2, :],
                                 cond=new).then_inc(s_w13in[c], 16)
            if not isinstance(s, int) or s >= 3:
                store_y(s - 3)
                sp.dma_start(y_dram[bass.ds((s - 3) * P, P), :], y_row[:, (j + 1) % UN, :]).then_inc(
                    s_yst[(j + 1) % UN], 16)

        def store_y(s):
            sp.wait_ge(s_mya, s + 1)
            sp.wait_ge(s_myv, s + 1)

        expert_turns(sp, body)
        for s in range(SLOT_TILES - 3, SLOT_TILES):
            store_y(s)
            sp.dma_start(y_dram[s * P:(s + 1) * P, :], y_row[:, s % UN, :]).then_inc(s_yst[s % UN], 16)
        sp.wait_ge(phase_end, 16)
        sp.dma_start(fin_b, final_norm.rearrange("(a n) -> a n", a=1).to_broadcast([P, D])).then_inc(s_fin_w, 16)

        def load_res(t):
            R = ROWS[t]
            if t >= FB:
                sp.wait_ge(s_yo, t - FB + 1)
            sp.dma_start(res[0:R, t % FB, :], h1_dram[t * P:t * P + R, :]).then_inc(s_res[t % FB], 16)

        sp.wait_ge(s_h1st, 16 * NT)
        for t in range(FB):
            load_res(t)
        for t in range(NT):
            R = ROWS[t]
            sp.wait_ge(s_yo, t + 1)
            if t < 8:
                sp.dma_start(y_prompt[0, t * P:(t + 1) * P, :], y_out[:, t % FB, :]).then_inc(s_yout[t % FB], 16)
            else:
                sp.dma_start(y_sample[0], y_out[0:SAMPLE, t % FB, :]).then_inc(s_yout[t % FB], 16)
            if t + FB < NT:
                load_res(t + FB)
        for j in range(FB):
            sp.wait_ge(s_yout[j], 16 * len(range(j, NT, FB)))

    def moe_pool(pool, rsqrt_mean):
        pool.wait_ge(s_slots, 2)
        pool.wait_ge(s_tokz, 16)
        for t in range(NT):
            for k in range(2):
                pool.indirect_dma_start(
                    out=tok_dram, out_offset=bass.IndirectOffsetOnAxis(ap=slot_i[0:ROWS[t], k, t:t + 1], axis=0),
                    in_=tab[0:ROWS[t], C_TOK + t:C_TOK + t + 1], in_offset=None).then_inc(s_scat, 16)
        pool.wait_ge(s_toki, 1)
        pool.wait_ge(s_hnst, 16 * NT)

        def gather(s):
            if s >= UN:
                pool.wait_ge(s_mx, s - UN + 1)
            pool.indirect_dma_start(
                out=xg[:, s % UN, :], out_offset=None, in_=hn_dram,
                in_offset=bass.IndirectOffsetOnAxis(ap=tok_i[:, s:s + 1], axis=0)).then_inc(s_xg[s % UN], 16)

        def load_second(s):
            e, new = expert(pool, s)
            for c in range(2):
                if s:
                    pool.wait_ge(s_w2lo, 2 * s + c - 1)
                pool.dma_start(w2_in[:, c], w2[0, bass.ds(e, 1), c * P:(c + 1) * P].rearrange("e p n -> p (e n)"),
                               cond=new).then_inc(s_w2in[c], 16)

        gather(0)
        load_second(0)
        gather(1)
        for s in range(SLOT_TILES):
            for c in range(2):
                pool.wait_ge(s_w2hi, 2 * s + c + 1)
                pool.tensor_tensor(w2_lo[s % UN][:, c], w2_in[:, c], w2_hi[s % UN][:, c].bitcast(F32),
                                   ALU.subtract).then_inc(s_w2lo, 1)
            if s + 1 < SLOT_TILES:
                load_second(s + 1)
            if s + UN < SLOT_TILES:
                gather(s + UN)
        end_phase(pool, 3)
        for j in range(UN):
            pool.wait_ge(s_yst[j], 16 * uses(j))

        def fetch(t):
            if t >= FB:
                pool.wait_ge(s_comb, t - FB + 1)
            for k, dst in enumerate((ya, yb)):
                pool.indirect_dma_start(
                    out=dst[0:ROWS[t], t % FB, :], out_offset=None, in_=y_dram,
                    in_offset=bass.IndirectOffsetOnAxis(ap=slot_i[0:ROWS[t], k, t:t + 1], axis=0)
                    ).then_inc(s_yab[t % FB], 16)

        for t in range(FB):
            fetch(t)
        for t in range(NT):
            R = ROWS[t]
            rsqrt_mean(y_stat[0:R, 1, t:t + 1], y_stat[0:R, 0, t:t + 1], D, s_ysq, s_yrs, t + 1)
            if t + FB < NT:
                fetch(t + FB)

    def moe_act(act):
        act.wait_ge(s_rexp_in, 1)
        act.activation(rt[:, 8, 0:45], rt[:, 8, 0:45], ACT.Exp).then_inc(s_rexp, 1)

        def split_weights(s, j):
            for c in range(WC):
                act.wait_ge(s_w13in[c], 32 * (s + 1))
                if c == 0 and not (isinstance(s, int) and s < UN):
                    act.wait_ge(s_mh, s - UN + 1)
                act.activation(chunk(w13_hi[j], c), chunk(w13_in, c), ACT.Copy).then_inc(s_w13hi, 1)

        def turned(s):
            act.wait_ge(s_mx, s + 1)
            if not is_zero(s):
                act.wait_ge(s_mh, s)
            for half in range(2):
                act.activation(xg_hi[:, 4 * half:4 * half + 4, :],
                               ps[:, half, :].rearrange("p (a b) -> p a b", a=4), ACT.Copy).then_inc(s_mxa, 1)

        def y_half(s, j):
            act.wait_ge(s_my, s + 1)
            return act.activation(y_row[:, j, 0:512], ps[:, 6, :], ACT.Copy).then_inc(s_mya, 1)

        def split_second(s, j):
            if not (isinstance(s, int) and s < UN):
                act.wait_ge(s_my, s - UN + 1)
            for c in range(2):
                act.wait_ge(s_w2in[c], 16 * (s + 1))
                act.activation(w2_hi[j][:, c], w2_in[:, c], ACT.Copy).then_inc(s_w2hi, 1)

        split_weights(0, 0)
        turned(0)
        split_second(0, 0)

        def body(it, j, first, last):
            s = it * UN + j
            start = first and j == 0
            if not last:
                split_weights(s + 1, (j + 1) % UN)
            act.wait_ge(s_mh, s + 1)
            if not start:
                act.wait_ge(s_mg, s)
            act.activation(act_h, ps[:, 3 + j, 0:FF], ACT.Silu).then_inc(s_ms, 1)
            if not last:
                turned(s + 1)
            if not start:
                if not first:
                    free_y(act, it, j)
                y_half(s - 1, (j - 1) % UN)
            act.wait_ge(s_mgt, s + 1)
            if not start:
                act.wait_ge(s_my, s)
            act.activation(g_hi, ps[:, 2, 0:2 * P].rearrange("p (a b) -> p a b", a=2),
                           ACT.Copy).then_inc(s_mga, 1)
            if not last:
                split_second(s + 1, (j + 1) % UN)

        expert_turns(act, body)
        free_last(act)
        y_half(SLOT_TILES - 1, (SLOT_TILES - 1) % UN)
        end_phase(act, 3)
        for t in range(NT):
            R = ROWS[t]
            act.wait_ge(s_comb, t + 1)
            if t:
                act.wait_ge(s_ysq, t)
            act.activation(y_sq[0:R], res[0:R, t % FB, :], ACT.Square,
                           accum_out=y_stat[0:R, 0, t:t + 1]).then_inc(s_ysq, 1)

    def free_y(eng, it, j):
        pj = (j - 1) % UN
        if j == 0:
            if isinstance(it, int) and it < 2:
                return
            n = it - 1
        else:
            n = it
        eng.wait_ge(s_yst[pj], n * 16)

    def free_last(eng):
        s = SLOT_TILES - 1
        eng.wait_ge(s_yst[s % UN], s // UN * 16)

    def moe_pe(pe):
        pe.wait_ge(s_cnt, 1)
        pe.matmul(ps[:, 0, 0:NT * NE], tab[:, C_TRI:C_TRI + P], rt[:, 15, :], start=True, stop=True)
        pe.matmul(ps[:, 1, 0:NT * NE], ones, rt[:, 15, :], start=True, stop=True).then_inc(s_rank, 1)
        pe.wait_ge(s_tokr, 16)
        pe.transpose(ps[:, 2, 0:SLOT_TILES], tok_rows[0:SLOT_TILES, :],
                     ident[0:SLOT_TILES, 0:SLOT_TILES]).then_inc(s_tokt, 1)

        def product(out, parts, w, start, stop):
            (x_hi, x_lo), (w_hi, w_lo) = parts, w
            pe.matmul(out, x_hi, w_hi, start=start, stop=False)
            pe.matmul(out, x_hi, w_lo, start=False, stop=False)
            return pe.matmul(out, x_lo, w_hi, start=False, stop=stop)

        def turn(s, it, j):
            pe.wait_ge(s_xg[j], 16 * (it + 1))
            if not is_zero(s):
                pe.wait_ge(s_mxa, 2 * s)
                pe.wait_ge(s_mxv, 2 * s)
            for kc in range(KC):
                ins = pe.transpose(ps[:, kc // 4, (kc % 4) * P:(kc % 4 + 1) * P], xg[:, j, kc * P:(kc + 1) * P], ident)
            ins.then_inc(s_mx, 1)

        def down(s, j):
            pe.wait_ge(s_mga, s + 1)
            pe.wait_ge(s_mgv, s + 1)
            pe.wait_ge(s_w2hi, 2 * s + 2)
            pe.wait_ge(s_w2lo, 2 * s + 2)
            if not is_zero(s):
                pe.wait_ge(s_mya, s)
                pe.wait_ge(s_myv, s)
            for n in range(2):
                cols = slice(n * 512, (n + 1) * 512)
                for c in range(2):
                    ins = product(ps[:, 6 + n, :], (g_hi[:, c, :], g_lo[:, c, :]),
                                  (w2_hi[j][:, c, cols], w2_lo[j][:, c, cols]), c == 0, c == 1)
            ins.then_inc(s_my, 1)

        pe.wait_ge(s_toki, 1)
        turn(0, 0, 0)

        def body(it, j, first, last):
            s = it * UN + j
            start = first and j == 0
            if not first:
                pe.wait_ge(s_mg, s - UN + 1)
            for kc in range(KC):
                if kc % 4 == 0:
                    pe.wait_ge(s_mxa, 2 * s + kc // 4 + 1)
                    pe.wait_ge(s_mxv, 2 * s + kc // 4 + 1)
                if kc % 2 == 0:
                    pe.wait_ge(s_w13hi, WC * s + kc // 2 + 1)
                    pe.wait_ge(s_w13lo, WC * s + kc // 2 + 1)
                ins = product(ps[:, 3 + j, :], (xg_hi[:, kc, :], xg_lo[:, kc, :]),
                              (w13_hi[j][:, kc, :], w13_lo[j][:, kc, :]), kc == 0, kc == KC - 1)
            ins.then_inc(s_mh, 1)
            if not last:
                turn(s + 1, it + (j + 1) // UN, (j + 1) % UN)
            if not start:
                down(s - 1, (j - 1) % UN)
            pe.wait_ge(s_mg, s + 1)
            if not start:
                pe.wait_ge(s_mga, s)
                pe.wait_ge(s_mgv, s)
            for c in range(2):
                ins = pe.transpose(ps[:, 2, c * P:(c + 1) * P], g_row[:, c * P:(c + 1) * P], ident)
            ins.then_inc(s_mgt, 1)

        expert_turns(pe, body)
        down(SLOT_TILES - 1, (SLOT_TILES - 1) % UN)
        end_phase(pe, 3)

    def moe_dve(dve, link):
        row = lambda k: rt[:, k, :]
        v9 = lambda k, n: rt[:, k, 0:NT * n].rearrange("p (t n) -> p t n", t=NT)
        col = lambda k: rt[:, k, 0:NT]
        w4 = tab[:, C_W4:C_W4 + 4].unsqueeze(1).to_broadcast([P, NT, 4])
        dve.memset(tok_rows, 0.0).then_inc(s_tok0, 1)

        def bc(x, n):
            return x.unsqueeze(2).to_broadcast([P, NT, n])

        def first_max(x, m, oh, tmp, tmp1):
            link(dve.tensor_reduce(m, x, AX.X, ALU.max))
            link(dve.tensor_tensor(tmp, x, bc(m, 4), ALU.is_equal))
            link(dve.tensor_tensor(tmp, tmp, w4, ALU.mult))
            link(dve.tensor_reduce(tmp1, tmp, AX.X, ALU.max))
            link(dve.tensor_tensor(oh, tmp, bc(tmp1, 4), ALU.is_equal))

        lg = logits[:, :, 0:NG]
        le = logits[:, :, NG:]
        oh_g, oh_1, oh_2, tmp, sel = v9(0, 4), v9(1, 4), v9(2, 4), v9(3, 4), v9(4, 4)
        m_g, m_1, m_2, t1 = col(5), col(6), col(7), col(9)
        first_max(lg, m_g, oh_g, tmp, t1)
        t16 = rt[:, 10, :].rearrange("p (t g j) -> p t g j", t=NT, g=NG)
        link(dve.tensor_tensor(t16, le.rearrange("p t (g j) -> p t g j", g=NG),
                               oh_g.unsqueeze(3).to_broadcast([P, NT, NG, EG]), ALU.mult))
        link(dve.tensor_reduce(sel, t16.rearrange("p t g j -> p t j g"), AX.X, ALU.add))
        first_max(sel, m_1, oh_1, tmp, t1)
        link(dve.scalar_tensor_tensor(out=sel, in0=oh_1, scalar=-3e38, in1=sel, op0=ALU.mult, op1=ALU.add))
        first_max(sel, m_2, oh_2, tmp, t1)
        link(dve.tensor_tensor(rt[:, 8, 0:36].rearrange("p (t n) -> p t n", t=NT), lg, bc(m_g, 4), ALU.subtract))
        dve.tensor_tensor(rt[:, 8, 36:45], m_2, m_1, ALU.subtract).then_inc(s_rexp_in, 1)
        valid = bc(tab[:, C_VALID:C_VALID + NT], NE)
        for k, oh in ((13, oh_1), (14, oh_2)):
            link(dve.tensor_tensor(rt[:, k, :].rearrange("p (t g j) -> p t g j", t=NT, g=NG),
                                   oh_g.unsqueeze(3).to_broadcast([P, NT, NG, EG]),
                                   oh.unsqueeze(2).to_broadcast([P, NT, NG, EG]), ALU.mult))
            link(dve.tensor_tensor(v9(k, NE), v9(k, NE), valid, ALU.mult))
        dve.tensor_tensor(row(15), row(13), row(14), ALU.add).then_inc(s_cnt, 1)
        dve.wait_ge(s_rexp, 1)
        link(dve.tensor_reduce(t1, rt[:, 8, 0:36].rearrange("p (t n) -> p t n", t=NT), AX.X, ALU.add))
        link(dve.reciprocal(t1, t1))
        link(dve.tensor_scalar(col(11), rt[:, 8, 36:45], 1.0, None, ALU.add))
        link(dve.reciprocal(col(11), col(11)))
        link(dve.tensor_tensor(gates[:, 0, :], t1, col(11), ALU.mult))
        link(dve.tensor_tensor(gates[:, 1, :], gates[:, 0, :], rt[:, 8, 36:45], ALU.mult))
        dve.wait_ge(s_rank, 1)
        base = v9(16, NE)
        link(dve.memset(base[:, 0, :], 0.0))
        for t in range(NT - 1):
            link(dve.tensor_tensor(base[:, t + 1, :], base[:, t, :], ps[:, 1, t * NE:(t + 1) * NE], ALU.add))
        count, tiles, incl, offs, zero = (rt[:, 17, k * NE:(k + 1) * NE] for k in range(5))
        link(dve.tensor_tensor(count, base[:, NT - 1, :], ps[:, 1, (NT - 1) * NE:NT * NE], ALU.add))
        link(dve.memset(zero, 0.0))
        over = rt[:, 18, :].rearrange("p (e k) -> p e k", e=NE)
        link(dve.tensor_tensor(over, count.unsqueeze(2).to_broadcast([P, NE, 9]),
                               tab[:, C_THR:C_THR + 9].unsqueeze(1).to_broadcast([P, NE, 9]), ALU.is_gt))
        link(dve.tensor_reduce(tiles, over, AX.X, ALU.add))
        link(dve.tensor_tensor_scan(incl, tiles, zero, 0.0, ALU.add, ALU.add))
        link(dve.tensor_tensor(offs, incl, tiles, ALU.subtract))
        link(dve.tensor_scalar(offs, offs, float(P), None, ALU.mult))
        link(dve.tensor_tensor(row(16), row(16), ps[:, 0, 0:NT * NE], ALU.add))
        link(dve.tensor_tensor(v9(16, NE), v9(16, NE), offs.unsqueeze(1).to_broadcast([P, NT, NE]), ALU.add))
        for k in range(2):
            link(dve.tensor_tensor(row(13 + k), row(13 + k), row(16), ALU.mult))
            link(dve.tensor_reduce(t1, v9(13 + k, NE), AX.X, ALU.add))
            dve.tensor_copy(slot_i[:, k, :], t1).then_inc(s_slots, 1)
            dve.wait_ge(s_slots, k + 1)
        le_tab = rt[:, 19:23, :].rearrange("p a b -> p (a b)")[:, 0:SLOT_TILES * NE].rearrange(
            "p (s e) -> p s e", s=SLOT_TILES)
        link(dve.tensor_tensor(le_tab, incl.unsqueeze(1).to_broadcast([P, SLOT_TILES, NE]),
                               tab[:, C_IOTA:C_IOTA + SLOT_TILES].unsqueeze(2).to_broadcast([P, SLOT_TILES, NE]),
                               ALU.is_le))
        link(dve.tensor_reduce(rt[:, 23, 0:SLOT_TILES], le_tab, AX.X, ALU.add))
        link(dve.tensor_scalar(rt[:, 23, 0:SLOT_TILES], rt[:, 23, 0:SLOT_TILES], float(NE - 1), None, ALU.min))
        dve.tensor_copy(expert_of, rt[:, 23, 0:SLOT_TILES]).then_inc(s_etab, 1)
        dve.wait_ge(s_tokt, 1)
        dve.tensor_copy(tok_i, ps[:, 2, 0:SLOT_TILES]).then_inc(s_toki, 1)

        def split_weights(s, j):
            for c in range(WC):
                dve.wait_ge(s_w13in[c], 32 * (s + 1))
                dve.wait_ge(s_w13hi, WC * s + c + 1)
                if c == 0 and not (isinstance(s, int) and s < UN):
                    dve.wait_ge(s_mh, s - UN + 1)
                dve.tensor_tensor(chunk(w13_lo[j], c), chunk(w13_in, c), chunk(w13_hi[j], c).bitcast(F32),
                                  ALU.subtract).then_inc(s_w13lo, 1)

        def turned(s):
            for half in range(2):
                dve.wait_ge(s_mxa, 2 * s + half + 1)
                if not is_zero(s):
                    dve.wait_ge(s_mh, s)
                hs = slice(4 * half, 4 * half + 4)
                dve.tensor_tensor(xg_lo[:, hs, :], ps[:, half, :].rearrange("p (a b) -> p a b", a=4),
                                  xg_hi[:, hs, :].bitcast(F32), ALU.subtract).then_inc(s_mxv, 1)

        def y_half(s, j):
            dve.wait_ge(s_my, s + 1)
            dve.tensor_copy(y_row[:, j, 512:1024], ps[:, 7, :]).then_inc(s_myv, 1)

        split_weights(0, 0)
        dve.wait_ge(s_mx, 1)
        turned(0)

        def body(it, j, first, last):
            s = it * UN + j
            start = first and j == 0
            if not last:
                split_weights(s + 1, (j + 1) % UN)
            dve.wait_ge(s_ms, s + 1)
            if not start:
                dve.wait_ge(s_mgt, s)
            dve.tensor_tensor(g_row, act_h, ps[:, 3 + j, FF:2 * FF], ALU.mult).then_inc(s_mg, 1)
            if not last:
                turned(s + 1)
            if not start:
                if not first:
                    free_y(dve, it, j)
                y_half(s - 1, (j - 1) % UN)
            dve.wait_ge(s_mga, s + 1)
            if not start:
                dve.wait_ge(s_my, s)
            dve.tensor_tensor(g_lo, ps[:, 2, 0:2 * P].rearrange("p (a b) -> p a b", a=2),
                              g_hi.bitcast(F32),
                              ALU.subtract).then_inc(s_mgv, 1)

        expert_turns(dve, body)
        free_last(dve)
        y_half(SLOT_TILES - 1, (SLOT_TILES - 1) % UN)
        end_phase(dve, 3)
        dve.wait_ge(s_fin_w, 16)

        def finish(t):
            R = ROWS[t]
            dve.wait_ge(s_yrs, t + 1)
            if t >= FB:
                dve.wait_ge(s_yout[t % FB], 16 * (t // FB))
            dve.scalar_tensor_tensor(out=y_out[0:R, t % FB, :], in0=res[0:R, t % FB, :], scalar=y_stat[0:R, 1, t:t + 1],
                                     in1=fin_b[0:R, :], op0=ALU.mult, op1=ALU.mult).then_inc(s_yo, 1)

        for t in range(NT):
            R = ROWS[t]
            dve.wait_ge(s_res[t % FB], 16 * (t // FB + 1))
            dve.wait_ge(s_yab[t % FB], 32 * (t // FB + 1))
            x = res[0:R, t % FB, :]
            link(dve.scalar_tensor_tensor(out=x, in0=ya[0:R, t % FB, :], scalar=gates[0:R, 0, t:t + 1], in1=x,
                                          op0=ALU.mult, op1=ALU.add))
            dve.scalar_tensor_tensor(out=x, in0=yb[0:R, t % FB, :], scalar=gates[0:R, 1, t:t + 1], in1=x,
                                     op0=ALU.mult, op1=ALU.add).then_inc(s_comb, 1)
            if t:
                finish(t - 1)
        finish(NT - 1)

    N_OUT = 2

    blk = ctx.enter_context(nc.Block())

    @blk.sync
    def _(sp):
        sp.dma_start(tab, table).then_inc(s_tab, 16)
        sp.dma_start(masks, level_masks).then_inc(s_tab, 16)
        sp.dma_start(an_b, attn_norm[0:1, :].to_broadcast([P, D])).then_inc(s_norm_w, 16)

        def load_x(t):
            if t >= 2:
                sp.wait_ge(s_xs, t - 1)
            if t < 8:
                sp.dma_start(x_row[:, t % 2, :], x_prompt[0, t * P:(t + 1) * P, :]).then_inc(s_xrow[t % 2], 32)
            else:
                sp.dma_start(x_row[0:SAMPLE, 0, :], x_sample[0]).then_inc(s_xrow[0], 16)
                sp.dma_start(x_row[SAMPLE:SAMPLE + META, 0, :], meta_tokens).then_inc(s_xrow[0], 16)

        def load_w(g):
            _, a, n = GROUPS[g]
            if g >= 2:
                sp.wait_ge(s_zps, sum(1 for z in Z_OUT if z[1] <= g - 2))
            sp.dma_start(w_grp[:, g % 2, :, 0:n],
                         w_in[0].rearrange("(c p) n -> p c n", p=P)[:, :, a:a + n]).then_inc(s_wg[g % 2], 16)

        load_x(0)
        load_x(1)
        load_w(0)
        load_w(1)
        for r_ in range(2):
            sp.dma_start(lbl[:, r_, :], hg_lb_logits[r_].rearrange("(h k) -> k h", k=HK),
                         allow_slow_non_contiguous=True).then_inc(s_hin, 16)
        sp.dma_start(gn_b, hg_gnorm[0:1, :].to_broadcast([P, HK])).then_inc(s_hin, 16)
        for t in range(2, NT):
            load_x(t)
        for g in range(2, len(GROUPS)):
            load_w(g)
        sp.wait_ge(phase_end, 4)
        sp.dma_start(state_s, state_hgrn[0, 0].rearrange("h k v -> k h v")).then_inc(s_st0, 16)
        sp.wait_ge(s_sev, 2)
        sp.dma_start(hgrn_sample[0, 0].rearrange("h k v -> k h v"), state_s).then_inc(s_out, 16)
        sp.wait_ge(s_sev, NT + 1)
        sp.dma_start(hgrn_prompt[0, 0].rearrange("h k v -> k h v"), state).then_inc(s_out, 16)
        attention_loads(sp)
        moe_loads(sp)
        sp.wait_ge(s_out, 16 * N_OUT)

    @blk.gpsimd
    def _(pool):
        def rsqrt_mean(out, ssq, n, before, after, count):
            pool.wait_ge(before, count)
            pool.tensor_scalar(out, ssq, 1.0 / n, EPS, ALU.mult, ALU.add).then_inc(s_pool, 1)
            pool_chain[0] += 1
            pool.wait_ge(s_pool, pool_chain[0])
            return pool.tensor_tensor(out, out, neg_half[0:out.shape[0], 0:out.shape[1]], ALU.pow).then_inc(after, 1)

        for n, (what, value) in enumerate([(z_mla[64:P, LAST, :], 0.0), (v_hg[64:P, LAST, :], 0.0),
                                           (hg_out[64:P, LAST, :], 0.0), (q_hg[:, :, T:TP], 0.0),
                                           (f_hg[:, :, T:TP], 1.0), (logits[64:P, LAST, :], 0.0)]):
            pool.memset(what, value).then_inc(s_zero, 1)
            pool.wait_ge(s_zero, n + 1)
        pool.wait_ge(s_tab, 32)
        for t in range(NT):
            rsqrt_mean(stat[0:ROWS[t], 16 + t:17 + t], stat[0:ROWS[t], t:t + 1], D, s_ssq, s_rstd, t + 1)
        pool.wait_ge(s_hin, 48)
        for t in range(NT):
            pool.wait_ge(s_zev, 2 * NT + t + 1)
            w = hg_out[:, t, :].rearrange("p (h v) -> p h v", h=HH)
            pool.tensor_tensor(w, w, gn_b.unsqueeze(1).to_broadcast([P, HH, HK]), ALU.mult).then_inc(s_gs, 1)
        end_phase(pool, 0)
        for i, c in enumerate(ORDER):
            rsqrt_mean(o_rstd[0:ROWS[c], i % 2, :], o_stat[0:ROWS[c], i % 2, :], HK, s_osq, s_ors, i + 1)
        end_phase(pool, 1)
        attention_pool(pool, rsqrt_mean)
        end_phase(pool, 2)
        moe_pool(pool, rsqrt_mean)

    @blk.scalar
    def _(act):
        act.wait_ge(s_tab, 32)
        for t in range(NT):
            act.wait_ge(s_xrow[t % 2], 32 * (t // 2 + 1))
            if t:
                act.wait_ge(s_ssq, t)
            act.activation(ps[0:ROWS[t], 0:2, :], x_row[0:ROWS[t], t % 2, :].rearrange("p (a b) -> p a b", a=2),
                           ACT.Square, accum_out=stat[0:ROWS[t], t:t + 1]).then_inc(s_ssq, 1)
            if t >= 1:
                x_half(act, t - 1)
        x_half(act, NT - 1)
        act.wait_ge(s_zero, 6)
        for n, (kind, g, m, k) in enumerate(Z_OUT):
            act.wait_ge(s_zps, n + 1)
            bank = n % Z_RING
            if kind == "mla":
                act.activation(z_mla[0:ROWS[m], m, :], ps[0:ROWS[m], bank, 0:ZA], ACT.Copy).then_inc(s_zev, 1)
            elif kind == "v":
                act.activation(v_hg[0:ROWS[m], m, :], ps[0:ROWS[m], bank, :], ACT.Copy).then_inc(s_zev, 1)
            elif kind == "gate":
                act.activation(hg_out[0:ROWS[m], m, :], ps[0:ROWS[m], bank, :], ACT.Silu).then_inc(s_zev, 1)
            elif kind == "f":
                act.activation(f_hg[:, m, k * ZN:(k + 1) * ZN], ps[:, bank, 0:ZN], ACT.Sigmoid).then_inc(s_zev, 1)
            else:
                act.activation(q_hg[:, m, k * ZN:(k + 1) * ZN], ps[:, bank, 0:ZN], ACT.Silu).then_inc(s_zev, 1)
        act.wait_ge(s_lb, 3)
        act.activation(lb[:, 0:2, :], lb[:, 0:2, :], ACT.Exp).then_inc(s_lbe, 1)
        end_phase(act, 0)
        for i, c in enumerate(ORDER):
            lv = levels(c)
            for n, h in enumerate(lv):
                k = LV0[i] + n
                nxt, cur = (k + 1) % 3, k % 3
                act.wait_ge(s_lvl, 2 * k + 2 * i + 2)
                if k >= 1:
                    act.wait_ge(s_cpy, 2 * k)
                if n >= 2:
                    act.wait_ge(s_prod, PR0[i] + n)
                a = q_lv[:, nxt].rearrange("p h (b u w) -> p h b u w", u=2, w=h)
                b = q_lv[:, cur].rearrange("p h (b u w) -> p h b u w", u=2, w=h)
                act.activation(a[:, :, :, 0, :], b[:, :, :, 0, :], ACT.Copy).then_inc(s_cpy, 1)
                a = k_lv[:, nxt].rearrange("p h (b u w) -> p h b u w", u=2, w=h)
                b = k_lv[:, cur].rearrange("p h (b u w) -> p h b u w", u=2, w=h)
                act.activation(a[:, :, :, 1, :], b[:, :, :, 1, :], ACT.Copy).then_inc(s_cpy, 1)
            act.wait_ge(s_ktp, i + 1)
            if i >= 1:
                act.wait_ge(s_sps, i)
            act.activation(k_rows, ps[:, 4, :].rearrange("p (h k) -> p h k", h=HH), ACT.Copy).then_inc(s_kte, 1)
            act.wait_ge(s_ops, i + 1)
            for hd in range(HH):
                ins = act.activation(ps[0:ROWS[c], 6, hd * P:(hd + 1) * P], ps[0:ROWS[c], 3, hd * P:(hd + 1) * P],
                                     ACT.Square, accum_out=o_stat[0:ROWS[c], i % 2, hd:hd + 1])
            ins.then_inc(s_osq, 1)
        end_phase(act, 1)
        attention_act(act)
        end_phase(act, 2)
        moe_act(act)

    @blk.tensor
    def _(pe):
        pe.wait_ge(s_tab, 32)
        for t in range(NT):
            pe.wait_ge(s_xs, t + 1)
            for half in range(2):
                if t:
                    pe.wait_ge(s_xta if half == 0 else s_xtv, t)
                for k in range(4):
                    kc = 4 * half + k
                    ins = pe.transpose(ps[:, 6 + half, k * P:k * P + ROWS[t]], xs[0:ROWS[t], 0, kc * P:(kc + 1) * P],
                                       ident[0:ROWS[t], 0:ROWS[t]])
                ins.then_inc(s_xps, 1)
        pe.wait_ge(s_xta, NT)
        pe.wait_ge(s_xtv, NT)
        for n, (kind, g, m, k) in enumerate(Z_OUT):
            if n == 0 or Z_OUT[n - 1][1] != g:
                pe.wait_ge(s_wg[g % 2], 16 * (g // 2 + 1))
            if n >= Z_RING:
                pe.wait_ge(s_zev, n - Z_RING + 1)
            w = w_grp[:, g % 2]
            bank = n % Z_RING
            for kc in range(KC):
                if kind in ("f", "q"):
                    ins = pe.matmul(ps[:, bank, 0:ZN], w[:, kc, m * P:(m + 1) * P], x_t[:, kc, k * ZN:(k + 1) * ZN],
                                    start=kc == 0, stop=kc == KC - 1)
                else:
                    nn = GROUPS[g][2]
                    ins = pe.matmul(ps[0:ROWS[m], bank, 0:nn], x_t[:, kc, col0(m):col0(m) + ROWS[m]], w[:, kc, 0:nn],
                                    start=kc == 0, stop=kc == KC - 1)
            ins.then_inc(s_zps, 1)
        end_phase(pe, 0)
        pe.wait_ge(s_st0, 16)
        for i, c in enumerate(ORDER):
            lv = levels(c)
            cs = slice(col0(c), col0(c) + P)
            for n in range(len(lv) + 1):
                pr = PR0[i] + n
                bank = pr % 3
                if pr >= 3:
                    pe.wait_ge(s_mask, pr - 2)
                if n == 0:
                    for hd in range(HH):
                        ins = pe.matmul(ps[:, bank, hd * P:(hd + 1) * P], k_hg[:, hd, cs], q_hg[:, hd, cs],
                                        start=True, stop=True)
                else:
                    h = lv[n - 1]
                    k = LV0[i] + n - 1
                    pe.wait_ge(s_lvl, 2 * k + 2 * i + 2)
                    if k:
                        pe.wait_ge(s_cpy, 2 * k)
                    for hd in range(HH):
                        tq = q_lv[:, k % 3, hd, :].rearrange("p (b u w) -> p b u w", u=2, w=h)[:, :, 1, :]
                        ins = pe.matmul(ps[:, bank, hd * 64:(hd + 1) * 64], k_lv[:, k % 3, hd, :], tq,
                                        start=True, stop=True)
                ins.then_inc(s_prod, 1)
            fin = (LV0[i] + len(lv)) % 3
            pe.wait_ge(s_lvl, 2 * LV0[i + 1] + 2 * i + 2)
            pe.wait_ge(s_cpy, 2 * LV0[i + 1])
            if i:
                pe.wait_ge(s_kte, i)
            for hd in range(HH):
                ins = pe.transpose(ps[:, 4, hd * P:(hd + 1) * P], k_lv[:, fin, hd, :], ident)
            ins.then_inc(s_ktp, 1)
            pe.wait_ge(s_mask, PR0[i + 1])
            if i:
                pe.wait_ge(s_oev, i)
                pe.wait_ge(s_sev, i + 1)
            R = ROWS[c]
            for hd in range(HH):
                o = ps[:, 3, hd * P:(hd + 1) * P]
                pe.matmul(o[0:R], attn_t[0:R, i % 2, hd, 0:R], v_hg[0:R, c, hd * P:(hd + 1) * P],
                          start=hd == 0, stop=False, skip_group_check=True)
                if c == LAST:
                    ins = pe.matmul(o[0:SAMPLE], q_lv[:, fin, hd, 0:SAMPLE], state_s[:, hd, :],
                                    start=False, stop=True, skip_group_check=True)
                else:
                    ins = pe.matmul(o[0:R], q_lv[:, fin, hd, :], state[:, hd, :],
                                    start=False, stop=True, skip_group_check=True)
            ins.then_inc(s_ops, 1)
            pe.wait_ge(s_kte, i + 1)
            for hd in range(HH):
                vv = v_hg[:, c, hd * P:(hd + 1) * P]
                if c == LAST:
                    pe.matmul(ps[:, 5, hd * P:(hd + 1) * P], k_rows[0:SAMPLE, hd, :], vv[0:SAMPLE],
                              start=True, stop=True)
                    ins = pe.matmul(ps[:, 7, hd * P:(hd + 1) * P], k_rows[SAMPLE:SAMPLE + META, hd, :],
                                    vv[SAMPLE:SAMPLE + META], start=True, stop=True)
                else:
                    ins = pe.matmul(ps[:, 5, hd * P:(hd + 1) * P], k_rows[:, hd, :], vv, start=True, stop=True)
            ins.then_inc(s_sps, 1)
        end_phase(pe, 1)
        attention_pe(pe)
        end_phase(pe, 2)
        moe_pe(pe)

    @blk.vector
    def _(dve):
        def link(ins):
            dve_chain[0] += 1
            ins.then_inc(s_dve, 1)
            dve.wait_ge(s_dve, dve_chain[0])

        dve.wait_ge(s_norm_w, 16)

        def second_half(t):
            dve.wait_ge(s_xps, 2 * t + 2)
            dve.tensor_copy(x_t[:, 4:8, col0(t):col0(t) + ROWS[t]],
                            ps[:, 7, :].rearrange("p (a b) -> p a b", a=4)[:, :, 0:ROWS[t]]).then_inc(s_xtv, 1)

        for t in range(NT):
            dve.wait_ge(s_rstd, t + 1)
            dve.wait_ge(s_xrow[t % 2], 32 * (t // 2 + 1))
            if t:
                dve.wait_ge(s_xps, 2 * t)
            R = ROWS[t]
            dve.scalar_tensor_tensor(out=xs[0:R, 0, :], in0=x_row[0:R, t % 2, :], scalar=stat[0:R, 16 + t:17 + t],
                                     in1=an_b[0:R, :], op0=ALU.mult, op1=ALU.mult).then_inc(s_xs, 1)
            second_half(t)
        dve.wait_ge(s_hin, 48)
        dve.tensor_tensor(lb[:, 2, :], lbl[:, 0, :], lbl[:, 1, :], ALU.max).then_inc(s_lb, 1)
        dve.wait_ge(s_lb, 1)
        dve.tensor_tensor(lb[:, 0, :], lbl[:, 0, :], lb[:, 2, :], ALU.subtract).then_inc(s_lb, 1)
        dve.tensor_tensor(lb[:, 1, :], lbl[:, 1, :], lb[:, 2, :], ALU.subtract).then_inc(s_lb, 1)
        dve.wait_ge(s_lbe, 1)
        link(dve.tensor_tensor(lb[:, 2, :], lb[:, 0, :], lb[:, 1, :], ALU.add))
        link(dve.reciprocal(lb[:, 2, :], lb[:, 2, :]))
        link(dve.tensor_tensor(lb[:, 0, :], lb[:, 0, :], lb[:, 2, :], ALU.mult))
        link(dve.tensor_scalar(lb[:, 1, :], lb[:, 0, :], -1.0, 1.0, ALU.mult, ALU.add))
        for hd in range(HH):
            link(dve.tensor_scalar(f_hg[:, hd, 0:T], f_hg[:, hd, 0:T], lb[:, 1, hd:hd + 1], lb[:, 0, hd:hd + 1],
                                   ALU.mult, ALU.add))
            dve.tensor_scalar(k_hg[:, hd, :], f_hg[:, hd, :], -1.0, 1.0, ALU.mult, ALU.add).then_inc(s_fk, 1)
        end_phase(dve, 0)
        link(dve.memset(state, 0.0))
        dve.wait_ge(s_st0, 16)
        for i, c in enumerate(ORDER):
            lv = levels(c)
            cs = slice(col0(c), col0(c) + P)
            R = ROWS[c]
            k0 = LV0[i]
            if i:
                dve.wait_ge(s_prod, PR0[i])
                dve.wait_ge(s_ops, i)
                dve.wait_ge(s_ktp, i)
            dve.scalar_tensor_tensor(out=q_lv[:, k0 % 3], in0=q_hg[:, :, cs], scalar=QSCALE, in1=f_hg[:, :, cs],
                                     op0=ALU.mult, op1=ALU.mult).then_inc(s_lvl, 1)
            dve.tensor_copy(k_lv[:, k0 % 3], k_hg[:, :, cs]).then_inc(s_lvl, 1)
            dve.wait_ge(s_prod, PR0[i] + 1)
            if i >= 2:
                dve.wait_ge(s_ops, i - 1)
            dve.tensor_tensor(attn_t[:, i % 2], ps[:, PR0[i] % 3, :].rearrange("p (h t) -> p h t", h=HH),
                                   ident_q.unsqueeze(1).to_broadcast([P, HH, P]), ALU.mult).then_inc(s_mask, 1)
            dve.wait_ge(s_mask, PR0[i] + 1)
            src_tot = f_hg[:, :, cs]
            for n, h in enumerate(lv):
                k = k0 + n
                nxt, cur = (k + 1) % 3, k % 3
                nb = P // (2 * h)
                pair = src_tot.rearrange("p h (b u) -> p h b u", u=2)
                dve.wait_ge(s_lvl, 2 * k + 2 * i + 2)
                if k:
                    dve.wait_ge(s_cpy, 2 * k)
                if n >= 2:
                    dve.wait_ge(s_prod, PR0[i] + n)
                a = q_lv[:, nxt].rearrange("p h (b u w) -> p h b u w", u=2, w=h)
                b = q_lv[:, cur].rearrange("p h (b u w) -> p h b u w", u=2, w=h)
                dve.tensor_tensor(a[:, :, :, 1, :], b[:, :, :, 1, :],
                                  pair[:, :, :, 0].unsqueeze(3).to_broadcast([P, HH, nb, h]),
                                  ALU.mult).then_inc(s_lvl, 1)
                a = k_lv[:, nxt].rearrange("p h (b u w) -> p h b u w", u=2, w=h)
                b = k_lv[:, cur].rearrange("p h (b u w) -> p h b u w", u=2, w=h)
                dve.tensor_tensor(a[:, :, :, 0, :], b[:, :, :, 0, :],
                                  pair[:, :, :, 1].unsqueeze(3).to_broadcast([P, HH, nb, h]),
                                  ALU.mult).then_inc(s_lvl, 1)
                nt = tot[:, n, :, 0:nb]
                link(dve.tensor_tensor(nt, pair[:, :, :, 0], pair[:, :, :, 1], ALU.mult))
                src_tot = nt
                pr = PR0[i] + n + 1
                dve.wait_ge(s_prod, pr + 1)
                out = attn_t[:, i % 2].rearrange("p h (b u w) -> p h b u w", u=2, w=h)
                where = masks[:, n * 64:(n + 1) * 64].rearrange("p (b w) -> p b w", w=h)
                dve.copy_predicated(
                    out[:, :, :, 1, :], where.unsqueeze(1).to_broadcast([P, HH, nb, h]),
                    ps[:, pr % 3, 0:HH * 64].rearrange("p (h b w) -> p h b w", h=HH, w=h)).then_inc(s_mask, 1)
            dve.wait_ge(s_sps, i + 1)
            if c == LAST:
                dve.wait_ge(s_ops, i + 1)
                for hd in range(HH):
                    ins = dve.scalar_tensor_tensor(out=state_s[:, hd, :], in0=state_s[:, hd, :],
                                                   scalar=src_tot[:, hd, 0:1],
                                                   in1=ps[:, 5, hd * P:(hd + 1) * P], op0=ALU.mult, op1=ALU.add)
                ins.then_inc(s_sev, 1)
                dve.tensor_copy(state, ps[:, 7, :].rearrange("p (h v) -> p h v", h=HH)).then_inc(s_sev, 1)
            else:
                dve.wait_ge(s_ops, i + 1)
                for hd in range(HH):
                    ins = dve.scalar_tensor_tensor(out=state[:, hd, :], in0=state[:, hd, :],
                                                   scalar=src_tot[:, hd, 0:1],
                                                   in1=ps[:, 5, hd * P:(hd + 1) * P], op0=ALU.mult, op1=ALU.add)
                ins.then_inc(s_sev, 1)
            dve.wait_ge(s_ors, i + 1)
            dve.wait_ge(s_gs, NT)
            for hd in range(HH):
                g_ = hg_out[0:R, c, hd * P:(hd + 1) * P]
                ins = dve.scalar_tensor_tensor(out=g_, in0=ps[0:R, 3, hd * P:(hd + 1) * P],
                                               scalar=o_rstd[0:R, i % 2, hd:hd + 1], in1=g_,
                                               op0=ALU.mult, op1=ALU.mult)
            ins.then_inc(s_oev, 1)
        end_phase(dve, 1)
        attention_dve(dve, link)
        end_phase(dve, 2)
        moe_dve(dve, link)

    ctx.close()


_INS = ["x_prompt", "x_sample", "cache_ckv", "cache_krope", "state_hgrn", "meta_tokens", "attn_norm", "w_in", "q_norm",
        "kv_norm", "w_uq", "w_uk", "w_uv", "hg_lb_logits", "hg_gnorm", "w_o", "ffn_norm", "w_router_group",
        "b_router_group", "w_router_expert", "b_router_expert", "w1", "w3", "w2", "final_norm"]
_OUTS = [(1, 1024, D), (1, SAMPLE, D), (1, 1, 1024 + META, CR), (1, 1, 1024 + META, RD), (1, 1, HH, HK, HK),
         (1, 1, SAMPLE, CR), (1, 1, SAMPLE, RD), (1, 1, HH, HK, HK)]


def kernel(**inputs):
    import numpy as np
    import concourse.bacc as bacc
    from concourse.bass_utils import run_bass_kernel_spmd

    nc = bacc.Bacc("TRN2", target_bir_lowering=False, num_devices=1)
    table, level_masks = constants()
    arrays, args = {}, []
    for name, a in [(n, np.ascontiguousarray(inputs[n])) for n in _INS] + [("table", table), ("masks", level_masks)]:
        arrays[f"in_{name}"] = a
        args.append(nc.dram_tensor(f"in_{name}", a.shape, mybir.dt.from_np(a.dtype), kind="ExternalInput").ap())
    for i, shape in enumerate(_OUTS):
        args.append(nc.dram_tensor(f"out_{i}", shape, F32, kind="ExternalOutput").ap())
    hybrid_layer(nc, *args)
    r = run_bass_kernel_spmd(nc, [arrays], core_ids=[0])
    return tuple(r.results[0][f"out_{i}"] for i in range(len(_OUTS)))
```
